# Optimizing a Trainium2 kernel written in Bass

```python
import math
import jax
import jax.numpy as jnp
from jax import lax
import numpy as np
import jax, jax.numpy as jnp

D_MODEL = 1024
BATCH = 1
SEQ = 256
DEPTH = 2

GRID_W = 64
CTX_LEN = 256
EPS = 1e-6
NEG_INF = -1e30
ROPE_THETA = 10000.0
Q_BLOCK = 128

DA_HEADS = 4
DA_HEAD_DIM = 64
DA_QK_WIDTH = DA_HEADS * 2 * DA_HEAD_DIM
DA_V_WIDTH = DA_HEADS * 2 * DA_HEAD_DIM
ROPE_AXIS = DA_HEAD_DIM // 2
ROPE_HALF = ROPE_AXIS // 2

SG_CHUNK = 128
SG_GROUPS = 4
SG_WIDTH = 512
SG_GROUP_DIM = SG_WIDTH // SG_GROUPS

NA_HEADS = 8
NA_HEAD_DIM = 64
NA_WIDTH = NA_HEADS * NA_HEAD_DIM
NA_ROWS_MAX = 8
NA_COLS = 16

N_BRANCH = 3
BRANCH_WIDTH = 512

OFF_KA = 0
OFF_VA = OFF_KA + DA_QK_WIDTH
OFF_KC = OFF_VA + DA_V_WIDTH
OFF_VC = OFF_KC + NA_WIDTH
KV_COLS = OFF_VC + NA_WIDTH
OFF_QA = KV_COLS
OFF_QC = OFF_QA + DA_QK_WIDTH
OFF_ZB = OFF_QC + NA_WIDTH
OFF_GATE = OFF_ZB + 2 * SG_WIDTH
IN_COLS = OFF_GATE + N_BRANCH * D_MODEL

N_GROUPS = 4
EXPERTS_PER_GROUP = 8
N_EXPERTS = N_GROUPS * EXPERTS_PER_GROUP
TOP_K = 2
D_EXPERT = 512
MOE_BLOCK = 128


def rms_norm(x, g):
    xf = x.astype(jnp.float32)
    y = xf * lax.rsqrt(jnp.mean(xf * xf, axis=-1, keepdims=True) + EPS)
    return (y * g.astype(jnp.float32)).astype(x.dtype)

def layer_norm(x, g, b):
    xf = x.astype(jnp.float32)
    mu = jnp.mean(xf, axis=-1, keepdims=True)
    var = jnp.mean(jnp.square(xf - mu), axis=-1, keepdims=True)
    y = (xf - mu) * lax.rsqrt(var + EPS)
    return (y * g.astype(jnp.float32) + b.astype(jnp.float32)).astype(x.dtype)

def ada_modulation(cond, w, b):
    m = cond @ w + b
    return jnp.split(m[:, None, :], 6, axis=-1)

def modulate(xn, shift, scale):
    return xn * (1.0 + scale) + shift

def da_qk_heads(t):
    return t.reshape(*t.shape[:-1], DA_HEADS, 2, DA_HEAD_DIM)

def da_v_heads(t):
    return t.reshape(*t.shape[:-1], DA_HEADS, 2 * DA_HEAD_DIM)

def na_heads(t):
    return t.reshape(*t.shape[:-1], NA_HEADS, NA_HEAD_DIM)

def axial_rope_tables(n_tok):
    t = jnp.arange(n_tok, dtype=jnp.int32)
    row = (t // GRID_W).astype(jnp.float32)
    col = (t % GRID_W).astype(jnp.float32)
    inv = ROPE_THETA ** (-jnp.arange(ROPE_HALF, dtype=jnp.float32) / ROPE_HALF)
    ar = row[:, None] * inv
    ac = col[:, None] * inv
    ang = jnp.concatenate([ar, ar, ac, ac], axis=-1)
    return jnp.cos(ang), jnp.sin(ang)

def apply_axial_rope(x, cos, sin):
    x1, x2, x3, x4 = jnp.split(x, 4, axis=-1)
    rot = jnp.concatenate([-x2, x1, -x4, x3], axis=-1)
    cos = cos[None, :, None, None, :].astype(x.dtype)
    sin = sin[None, :, None, None, :].astype(x.dtype)
    return x * cos + rot * sin

def diff_softmax_mix(q, k, v, lam):
    s = jnp.einsum('bqhmd,bkhmd->bhmqk', q, k).astype(jnp.float32) * (DA_HEAD_DIM ** -0.5)
    p = jax.nn.softmax(s, axis=-1)
    w = (p[:, :, 0] - lam * p[:, :, 1]).astype(v.dtype)
    return jnp.einsum('bhqk,bkhe->bqhe', w, v)

def diff_attention_latent(q, k, v, k_ctx, v_ctx, lam):
    b, n = q.shape[:2]
    k_all = jnp.concatenate([k_ctx, k], axis=1)
    v_all = jnp.concatenate([v_ctx, v], axis=1)
    qb = q.reshape(b, n // Q_BLOCK, Q_BLOCK, DA_HEADS, 2, DA_HEAD_DIM).swapaxes(0, 1)
    o = lax.map(lambda qq: diff_softmax_mix(qq, k_all, v_all, lam), qb)
    return o.swapaxes(0, 1).reshape(b, n, DA_HEADS, 2 * DA_HEAD_DIM)

def diff_post(o, g, lam_init):
    y = rms_norm(o, g) * (1.0 - lam_init)
    return y.reshape(*o.shape[:2], DA_V_WIDTH)

def spatial_gating(z, ln_g, ln_b, w_s, b_s):
    z = jax.nn.gelu(z)
    u, vv = jnp.split(z, 2, axis=-1)
    vv = layer_norm(vv, ln_g, ln_b)
    b, n, _ = vv.shape
    vv = vv.reshape(b, n // SG_CHUNK, SG_CHUNK, SG_GROUPS, SG_GROUP_DIM)
    s = jnp.einsum('gpq,bnqgc->bnpgc', w_s, vv) + b_s.T[None, None, :, :, None]
    return u * s.reshape(b, n, SG_WIDTH)

def neighbourhood_attention(q, k, v, k_ctx, v_ctx, rpb, rows):
    b, n, nh, dh = q.shape
    kr = min(NA_ROWS_MAX, rows)
    n_cb = GRID_W // NA_COLS
    half = NA_COLS // 2
    band_w = 2 * NA_COLS
    scale = dh ** -0.5

    def grid_padded(t):
        t = t.reshape(b, rows, GRID_W, nh, dh)
        return jnp.pad(t, ((0, 0), (0, 0), (half, half), (0, 0), (0, 0)))

    kg, vg = grid_padded(k), grid_padded(v)
    qcol = np.arange(GRID_W).reshape(n_cb, NA_COLS)
    kcol = np.arange(n_cb)[:, None] * NA_COLS - half + np.arange(band_w)[None, :]
    cstart = np.clip(qcol - half, 0, GRID_W - NA_COLS)
    col_ok = jnp.asarray((kcol[:, None, :] >= cstart[..., None]) & (kcol[:, None, :] < cstart[..., None] + NA_COLS))
    dc_idx = np.clip(kcol[:, None, :] - qcol[:, :, None] + NA_COLS - 1, 0, 2 * NA_COLS - 2)
    rpb_c = rpb.astype(jnp.float32)[:, :, dc_idx]

    def row_step(args):
        r, qr = args
        rs = jnp.clip(r - kr // 2, 0, rows - kr)

        def band(t):
            t = lax.dynamic_slice_in_dim(t, rs, kr, axis=1).reshape(b, kr, n_cb + 1, NA_COLS, nh, dh)
            return jnp.concatenate([t[:, :, :-1], t[:, :, 1:]], axis=3)

        kb, vb = band(kg), band(vg)
        qb = qr.reshape(b, n_cb, NA_COLS, nh, dh)
        s_win = jnp.einsum('bjqhd,brjkhd->bhjqrk', qb, kb).astype(jnp.float32) * scale
        dr_idx = rs + jnp.arange(kr) - r + NA_ROWS_MAX - 1
        bias = jnp.take(rpb_c, dr_idx, axis=1).transpose(0, 2, 3, 1, 4)
        s_win = jnp.where(col_ok[:, :, None, :], s_win + bias[None], NEG_INF)
        s_ctx = jnp.einsum('bjqhd,bkhd->bhjqk', qb, k_ctx).astype(jnp.float32) * scale
        nw = kr * band_w
        s = jnp.concatenate([s_win.reshape(b, nh, n_cb, NA_COLS, nw), s_ctx], axis=-1)
        p = jax.nn.softmax(s, axis=-1).astype(v.dtype)
        p_win = p[..., :nw].reshape(b, nh, n_cb, NA_COLS, kr, band_w)
        o = (jnp.einsum('bhjqrk,brjkhd->bjqhd', p_win, vb)
             + jnp.einsum('bhjqk,bkhd->bjqhd', p[..., nw:], v_ctx))
        return o.reshape(b, GRID_W, nh, dh)

    q_rows = q.reshape(b, rows, GRID_W, nh, dh).swapaxes(0, 1)
    o = lax.map(row_step, (jnp.arange(rows, dtype=jnp.int32), q_rows))
    return o.swapaxes(0, 1).reshape(b, n, nh * dh)

def ctx_attention(q, k, v):
    s = jnp.einsum('bqhd,bkhd->bhqk', q, k).astype(jnp.float32) * (q.shape[-1] ** -0.5)
    p = jax.nn.softmax(s, axis=-1).astype(v.dtype)
    o = jnp.einsum('bhqk,bkhd->bqhd', p, v)
    return o.reshape(*o.shape[:2], -1)

def merge_branches(p_gate, y_a, y_b, y_c, w_branch, w_out):
    ys = jnp.stack([y_a, y_b, y_c], axis=2)
    yb = jnp.einsum('bnie,ied->bnid', ys, w_branch)
    g = jax.nn.sigmoid(p_gate.reshape(*p_gate.shape[:-1], N_BRANCH, D_MODEL))
    return jnp.sum(g * yb, axis=2) @ w_out

def hier_moe(x, w_group, b_group, w_router, b_router, w_gate, w_up, w_down):
    t = x.shape[0]
    g_logits = (x @ w_group).astype(jnp.float32) + b_group.astype(jnp.float32)
    g_prob = jax.nn.softmax(g_logits, axis=-1)
    g_idx = jnp.argmax(g_logits, axis=-1)
    g_w = jnp.take_along_axis(g_prob, g_idx[:, None], axis=1)
    e_logits = ((x @ w_router).astype(jnp.float32) + b_router.astype(jnp.float32)).reshape(t, N_GROUPS, EXPERTS_PER_GROUP)
    e_logits = e_logits[jnp.arange(t), g_idx]
    top_l, top_i = lax.top_k(e_logits, TOP_K)
    top_w = jax.nn.softmax(top_l, axis=-1) * g_w
    expert = (g_idx[:, None] * EXPERTS_PER_GROUP + top_i).astype(jnp.int32)

    a = t * TOP_K
    flat_e = expert.reshape(a)
    order = jnp.argsort(flat_e).astype(jnp.int32)
    sorted_e = flat_e[order]
    counts = jnp.bincount(flat_e, length=N_EXPERTS)
    padded = (counts + MOE_BLOCK - 1) // MOE_BLOCK * MOE_BLOCK
    pad_end = jnp.cumsum(padded)
    pad_start = pad_end - padded
    start = jnp.cumsum(counts) - counts
    dest = pad_start[sorted_e] + jnp.arange(a, dtype=jnp.int32) - start[sorted_e]
    n_blocks = -(-(a + N_EXPERTS * (MOE_BLOCK - 1)) // MOE_BLOCK)
    n_slots = n_blocks * MOE_BLOCK
    slot_token = jnp.full((n_slots,), t, jnp.int32).at[dest].set(order // TOP_K)
    x_pad = jnp.concatenate([x, jnp.zeros((1, x.shape[1]), x.dtype)], axis=0)
    xs = x_pad[slot_token].reshape(n_blocks, MOE_BLOCK, x.shape[1])
    block_expert = jnp.minimum(jnp.searchsorted(pad_end, jnp.arange(n_blocks) * MOE_BLOCK, side='right'), N_EXPERTS - 1)

    def expert_block(args):
        xb, e = args
        hdn = jax.nn.silu(xb @ w_gate[e]) * (xb @ w_up[e])
        return hdn @ w_down[e]

    ys = lax.map(expert_block, (xs, block_expert)).reshape(n_slots, -1)
    w_sorted = top_w.reshape(a)[order].astype(ys.dtype)
    return jax.ops.segment_sum(ys[dest] * w_sorted[:, None], order // TOP_K, num_segments=t)

def first_inputs(seed: int = 0) -> dict:
    key = jax.random.key(seed)
    ks = jax.random.split(key, 32)
    f32 = jnp.float32
    D = D_MODEL

    def nrm(k, shape, scale):
        return jax.random.normal(k, shape, f32) * scale

    return {
        'x': nrm(ks[0], (BATCH, SEQ, D), 1.0),
        'c': nrm(ks[1], (BATCH, D), 1.0),
        'ctx': nrm(ks[2], (BATCH, CTX_LEN, D), 1.0),
        'c_ctx': nrm(ks[3], (D,), 1.0),
        'w_ada': nrm(ks[4], (DEPTH, D, 6 * D), 0.5 * D ** -0.5),
        'b_ada': nrm(ks[5], (DEPTH, 6 * D), 0.02),
        'g_norm_mix': 1.0 + nrm(ks[6], (DEPTH, D), 0.02),
        'g_norm_ffn': 1.0 + nrm(ks[7], (DEPTH, D), 0.02),
        'w_in': nrm(ks[8], (DEPTH, D, IN_COLS), D ** -0.5),
        'da_lambda': nrm(ks[9], (DEPTH, 4, DA_HEAD_DIM), 0.1),
        'da_subln_g': 1.0 + nrm(ks[10], (DEPTH, 2 * DA_HEAD_DIM), 0.02),
        'sg_ln_g': 1.0 + nrm(ks[11], (DEPTH, SG_WIDTH), 0.02),
        'sg_ln_b': nrm(ks[12], (DEPTH, SG_WIDTH), 0.02),
        'sg_w': nrm(ks[13], (DEPTH, SG_GROUPS, SG_CHUNK, SG_CHUNK), SG_CHUNK ** -0.5),
        'sg_b': 1.0 + nrm(ks[14], (DEPTH, SG_GROUPS, SG_CHUNK), 0.02),
        'na_rpb': nrm(ks[15], (DEPTH, NA_HEADS, 2 * NA_ROWS_MAX - 1, 2 * NA_COLS - 1), 0.1),
        'w_branch': nrm(ks[16], (DEPTH, N_BRANCH, BRANCH_WIDTH, D), BRANCH_WIDTH ** -0.5),
        'w_out': nrm(ks[17], (DEPTH, D, D), D ** -0.5),
        'moe_w_group': nrm(ks[18], (DEPTH, D, N_GROUPS), D ** -0.5),
        'moe_b_group': nrm(ks[19], (DEPTH, N_GROUPS), 0.01),
        'moe_w_router': nrm(ks[20], (DEPTH, D, N_EXPERTS), D ** -0.5),
        'moe_b_router': nrm(ks[21], (DEPTH, N_EXPERTS), 0.01),
        'moe_w_gate': nrm(ks[22], (DEPTH, N_EXPERTS, D, D_EXPERT), D ** -0.5),
        'moe_w_up': nrm(ks[23], (DEPTH, N_EXPERTS, D, D_EXPERT), D ** -0.5),
        'moe_w_down': nrm(ks[24], (DEPTH, N_EXPERTS, D_EXPERT, D), D_EXPERT ** -0.5),
        'g_final': 1.0 + nrm(ks[25], (D,), 0.02),
    }

def first_block(x, c, ctx, c_ctx, w_ada, b_ada, g_norm_mix, g_norm_ffn, w_in, da_lambda, da_subln_g,
              sg_ln_g, sg_ln_b, sg_w, sg_b, na_rpb, w_branch, w_out, moe_w_group, moe_b_group,
              moe_w_router, moe_b_router, moe_w_gate, moe_w_up, moe_w_down, g_final):
    b, n_lat, _ = x.shape
    n_ctx = ctx.shape[1]
    rows = n_lat // GRID_W
    cos, sin = axial_rope_tables(n_lat)
    cond_lat = jax.nn.silu(c)
    cond_ctx = jax.nn.silu(c_ctx)[None]
    h, hc = x, ctx
    for l in range(DEPTH):
        last = l == DEPTH - 1
        lam_init = 0.8 - 0.6 * math.exp(-0.3 * l)
        lq1, lk1, lq2, lk2 = da_lambda[l].astype(jnp.float32)
        lam = jnp.exp(jnp.sum(lq1 * lk1)) - jnp.exp(jnp.sum(lq2 * lk2)) + lam_init
        sh1, sc1, gt1, sh2, sc2, gt2 = ada_modulation(cond_lat, w_ada[l], b_ada[l])
        csh1, csc1, cgt1, csh2, csc2, cgt2 = ada_modulation(cond_ctx, w_ada[l], b_ada[l])

        xn = modulate(rms_norm(h, g_norm_mix[l]), sh1, sc1)
        xc = modulate(rms_norm(hc, g_norm_mix[l]), csh1, csc1)
        p = xn @ w_in[l]
        pc = xc @ (w_in[l][:, :KV_COLS] if last else w_in[l])
        ka_c = da_qk_heads(pc[..., OFF_KA:OFF_VA])
        va_c = da_v_heads(pc[..., OFF_VA:OFF_KC])
        kc_c = na_heads(pc[..., OFF_KC:OFF_VC])
        vc_c = na_heads(pc[..., OFF_VC:KV_COLS])

        qa = apply_axial_rope(da_qk_heads(p[..., OFF_QA:OFF_QC]), cos, sin)
        ka = apply_axial_rope(da_qk_heads(p[..., OFF_KA:OFF_VA]), cos, sin)
        va = da_v_heads(p[..., OFF_VA:OFF_KC])
        y_a = diff_post(diff_attention_latent(qa, ka, va, ka_c, va_c, lam), da_subln_g[l], lam_init)
        y_b = spatial_gating(p[..., OFF_ZB:OFF_GATE], sg_ln_g[l], sg_ln_b[l], sg_w[l], sg_b[l])
        y_c = neighbourhood_attention(na_heads(p[..., OFF_QC:OFF_ZB]), na_heads(p[..., OFF_KC:OFF_VC]),
                                      na_heads(p[..., OFF_VC:KV_COLS]), kc_c, vc_c, na_rpb[l], rows)
        h = h + gt1 * merge_branches(p[..., OFF_GATE:], y_a, y_b, y_c, w_branch[l], w_out[l])
        if not last:
            ya_c = diff_post(diff_softmax_mix(da_qk_heads(pc[..., OFF_QA:OFF_QC]), ka_c, va_c, lam), da_subln_g[l], lam_init)
            yb_c = spatial_gating(pc[..., OFF_ZB:OFF_GATE], sg_ln_g[l], sg_ln_b[l], sg_w[l], sg_b[l])
            yc_c = ctx_attention(na_heads(pc[..., OFF_QC:OFF_ZB]), kc_c, vc_c)
            hc = hc + cgt1 * merge_branches(pc[..., OFF_GATE:], ya_c, yb_c, yc_c, w_branch[l], w_out[l])

        xn2 = modulate(rms_norm(h, g_norm_ffn[l]), sh2, sc2).reshape(b * n_lat, D_MODEL)
        if last:
            y = hier_moe(xn2, moe_w_group[l], moe_b_group[l], moe_w_router[l], moe_b_router[l],
                         moe_w_gate[l], moe_w_up[l], moe_w_down[l])
            h = h + gt2 * y.reshape(b, n_lat, D_MODEL)
        else:
            xc2 = modulate(rms_norm(hc, g_norm_ffn[l]), csh2, csc2).reshape(b * n_ctx, D_MODEL)
            y = hier_moe(jnp.concatenate([xn2, xc2], axis=0), moe_w_group[l], moe_b_group[l],
                         moe_w_router[l], moe_b_router[l], moe_w_gate[l], moe_w_up[l], moe_w_down[l])
            h = h + gt2 * y[:b * n_lat].reshape(b, n_lat, D_MODEL)
            hc = hc + cgt2 * y[b * n_lat:].reshape(b, n_ctx, D_MODEL)
    return rms_norm(h, g_final)


DEPTH_2 = 1

BRANCH_WIDTH_2 = D_MODEL // 2
GLA_HEADS = 4
GLA_DV = BRANCH_WIDTH_2 // GLA_HEADS
GLA_DK = GLA_DV // 2
GLA_RANK = 16
GLA_TAU = 16.0
GLA_CHUNK = 16
GLA_QK = GLA_HEADS * GLA_DK
GLA_V = GLA_HEADS * GLA_DV
SC_WIDTH = BRANCH_WIDTH_2
CONV_K = 3
DIL_PATTERNS = ((128, 1), (512, 4), (2048, 16))
DIL_GROUPS = len(DIL_PATTERNS)
DIL_HEADS = 4
DIL_HD = BRANCH_WIDTH_2 // DIL_HEADS
DIL_W = DIL_GROUPS * DIL_HEADS * DIL_HD
DIL_BLOCK = 128
D_FF = 2816

IN_SIZES = (GLA_QK, GLA_QK, GLA_V, GLA_V, GLA_RANK,
            SC_WIDTH, SC_WIDTH, SC_WIDTH,
            DIL_W, DIL_W, DIL_W)
IN_COLS_2 = sum(IN_SIZES)


def rmsnorm(x, g):
    xf = x.astype(jnp.float32)
    r = lax.rsqrt(jnp.mean(xf * xf, axis=-1, keepdims=True) + EPS)
    return (xf * r).astype(x.dtype) * g

def causal_dwconv(u, w):
    K = w.shape[0]
    S = u.shape[1]
    up = jnp.pad(u, ((0, 0), (K - 1, 0), (0, 0)))
    y = w[0] * up[:, 0:S]
    for k in range(1, K):
        y = y + w[k] * up[:, k:k + S]
    return y

def rope(x, pos):
    hd = x.shape[-1]
    inv = ROPE_THETA ** (-jnp.arange(0, hd, 2, dtype=jnp.float32) / hd)
    ang = pos.astype(jnp.float32)[..., None] * inv
    cos = jnp.cos(ang)[:, :, None, None, :]
    sin = jnp.sin(ang)[:, :, None, None, :]
    xf = x.astype(jnp.float32)
    x1, x2 = xf[..., :hd // 2], xf[..., hd // 2:]
    return jnp.concatenate([x1 * cos - x2 * sin, x2 * cos + x1 * sin], axis=-1).astype(x.dtype)

def gla_branch(q, k, v, g, a_low, w_a_up, b_a, norm_g):
    B, S, _ = q.shape
    H, C = GLA_HEADS, GLA_CHUNK
    N = S // C
    f32 = jnp.float32
    loga = jax.nn.log_sigmoid((a_low.astype(f32) @ w_a_up.astype(f32)) + b_a.astype(f32)) / GLA_TAU

    def chunks(t, d):
        return t.astype(f32).reshape(B, N, C, H, d).transpose(0, 3, 1, 2, 4)

    qc = chunks(q, GLA_DK) * (GLA_DK ** -0.5)
    kc = chunks(k, GLA_DK)
    vc = chunks(v, GLA_DV)
    lc = jnp.cumsum(chunks(loga, GLA_DK), axis=3)

    causal = jnp.tril(jnp.ones((C, C), dtype=bool))
    rel = lc[..., :, None, :] - lc[..., None, :, :]
    decay = jnp.exp(jnp.where(causal[:, :, None], rel, -jnp.inf))
    scores = jnp.einsum('bhnid,bhnjd,bhnijd->bhnij', qc, kc, decay)
    o_intra = jnp.einsum('bhnij,bhnje->bhnie', scores, vc)

    lend = lc[..., -1:, :]
    q_in = qc * jnp.exp(lc)
    k_in = kc * jnp.exp(lend - lc)
    dec_chunk = jnp.exp(lend[..., 0, :])

    def step(state, xs):
        qn, kn, vn, dn = xs
        o = jnp.einsum('bhid,bhde->bhie', qn, state)
        state = state * dn[..., None] + jnp.einsum('bhjd,bhje->bhde', kn, vn)
        return state, o

    xs = (jnp.moveaxis(q_in, 2, 0), jnp.moveaxis(k_in, 2, 0),
          jnp.moveaxis(vc, 2, 0), jnp.moveaxis(dec_chunk, 2, 0))
    s0 = jnp.zeros((B, H, GLA_DK, GLA_DV), f32)
    _, o_inter = lax.scan(step, s0, xs)
    o = o_intra + jnp.moveaxis(o_inter, 0, 2)
    o = o.transpose(0, 2, 3, 1, 4).reshape(B, S, H, GLA_DV).astype(v.dtype)
    o = rmsnorm(o, norm_g).reshape(B, S, GLA_V)
    return o * jax.nn.silu(g)

def strided_window_attn(q, k, v, span, dil):
    B, S, H, D = q.shape
    L = S // dil
    BLK = DIL_BLOCK
    nb = -(-L // BLK)
    Lp = nb * BLK

    def to_sub(t):
        return t.reshape(B, L, dil, H, D).transpose(0, 2, 3, 1, 4)

    qs, ks, vs = to_sub(q), to_sub(k), to_sub(v)
    qb = jnp.pad(qs, ((0, 0), (0, 0), (0, 0), (0, Lp - L), (0, 0))).reshape(B, dil, H, nb, BLK, D)

    def kv_blocks(t):
        tp = jnp.pad(t, ((0, 0), (0, 0), (0, 0), (BLK, Lp - L), (0, 0)))
        prev = tp[:, :, :, :Lp].reshape(B, dil, H, nb, BLK, D)
        cur = tp[:, :, :, BLK:].reshape(B, dil, H, nb, BLK, D)
        return jnp.concatenate([prev, cur], axis=4)

    kb, vb = kv_blocks(ks), kv_blocks(vs)
    i = jnp.arange(BLK)[:, None]
    m = jnp.arange(2 * BLK)[None, :]
    blk = jnp.arange(nb)[:, None, None]
    dist = i + BLK - m
    key_idx = (blk - 1) * BLK + m
    valid = (dist >= 0) & (dist <= span) & (key_idx >= 0)

    s = jnp.einsum('brhnid,brhnmd->brhnim', qb, kb).astype(jnp.float32) * (D ** -0.5)
    s = jnp.where(valid, s, -jnp.inf)
    mx = jnp.max(s, axis=-1, keepdims=True)
    p = jnp.exp(s - mx)
    den = jnp.sum(p, axis=-1, keepdims=True)
    o = jnp.einsum('brhnim,brhnmd->brhnid', p, vb.astype(jnp.float32)) / den
    lse = (mx + jnp.log(den))[..., 0]

    o = o.reshape(B, dil, H, Lp, D)[:, :, :, :L].transpose(0, 3, 1, 2, 4).reshape(B, S, H, D)
    lse = lse.reshape(B, dil, H, Lp)[:, :, :, :L].transpose(0, 3, 1, 2).reshape(B, S, H)
    return o, lse

def dilated_branch(dq, dk, dv, pos):
    B, S, _ = dq.shape
    shp = (B, S, DIL_GROUPS, DIL_HEADS, DIL_HD)
    q = rope(dq.reshape(shp), pos)
    k = rope(dk.reshape(shp), pos)
    v = dv.reshape(shp)
    outs, lses = [], []
    for gi, (win, dil) in enumerate(DIL_PATTERNS):
        o, lse = strided_window_attn(q[:, :, gi], k[:, :, gi], v[:, :, gi], win // dil, dil)
        outs.append(o)
        lses.append(lse)
    w = jax.nn.softmax(jnp.stack(lses, axis=0), axis=0)
    o = jnp.sum(w[..., None] * jnp.stack(outs, axis=0), axis=0)
    return o.reshape(B, S, DIL_HEADS * DIL_HD).astype(dq.dtype)

def second_inputs(seed: int = 0) -> dict:
    key = jax.random.key(seed)
    ks = jax.random.split(key, 24)
    f32 = jnp.float32

    def nrm(k, shape, scale):
        return jax.random.normal(k, shape, f32) * scale

    def gain(k, shape):
        return 1.0 + 0.02 * jax.random.normal(k, shape, f32)

    x = jax.random.normal(ks[0], (BATCH, SEQ, D_MODEL), f32)
    offset = jax.random.randint(ks[1], (BATCH, 1), 0, 4096, dtype=jnp.int32)
    positions = (offset + jnp.arange(SEQ, dtype=jnp.int32)[None, :]).astype(jnp.int32)
    return {
        "x": x,
        "positions": positions,
        "w_in": nrm(ks[2], (DEPTH_2, D_MODEL, IN_COLS_2), D_MODEL ** -0.5),
        "w_alpha_up": nrm(ks[3], (DEPTH_2, GLA_RANK, GLA_QK), GLA_RANK ** -0.5),
        "b_alpha": nrm(ks[4], (DEPTH_2, GLA_QK), 0.1),
        "gla_norm_g": gain(ks[5], (DEPTH_2, GLA_DV)),
        "sc_conv_w": nrm(ks[6], (DEPTH_2, CONV_K, SC_WIDTH), CONV_K ** -0.5),
        "w_gate": nrm(ks[7], (DEPTH_2, D_MODEL, N_BRANCH * D_MODEL), D_MODEL ** -0.5),
        "b_gate": nrm(ks[8], (DEPTH_2, N_BRANCH * D_MODEL), 0.02),
        "w_branch": nrm(ks[9], (DEPTH_2, N_BRANCH, BRANCH_WIDTH_2, D_MODEL), BRANCH_WIDTH_2 ** -0.5),
        "w_mix_out": nrm(ks[10], (DEPTH_2, D_MODEL, D_MODEL), D_MODEL ** -0.5),
        "pre_mix_g": gain(ks[11], (DEPTH_2, D_MODEL)),
        "post_mix_g": gain(ks[12], (DEPTH_2, D_MODEL)),
        "pre_ffn_g": gain(ks[13], (DEPTH_2, D_MODEL)),
        "post_ffn_g": gain(ks[14], (DEPTH_2, D_MODEL)),
        "w_ff_gate": nrm(ks[15], (DEPTH_2, D_MODEL, D_FF), D_MODEL ** -0.5),
        "w_ff_up": nrm(ks[16], (DEPTH_2, D_MODEL, D_FF), D_MODEL ** -0.5),
        "ff_conv_w": nrm(ks[17], (DEPTH_2, CONV_K, D_FF), CONV_K ** -0.5),
        "ff_conv_b": nrm(ks[18], (DEPTH_2, D_FF), 0.02),
        "w_ff_down": nrm(ks[19], (DEPTH_2, D_FF, D_MODEL), D_FF ** -0.5),
    }

def second_block(x, positions, w_in, w_alpha_up, b_alpha, gla_norm_g, sc_conv_w, w_gate, b_gate,
              w_branch, w_mix_out, pre_mix_g, post_mix_g, pre_ffn_g, post_ffn_g,
              w_ff_gate, w_ff_up, ff_conv_w, ff_conv_b, w_ff_down):
    B, S, _ = x.shape
    split_points = np.cumsum(np.array(IN_SIZES))[:-1].tolist()
    for l in range(DEPTH_2):
        h = rmsnorm(x, pre_mix_g[l])
        z = h @ w_in[l]
        (g_q, g_k, g_v, g_o, a_low, sc_b, sc_c, sc_x,
         d_q, d_k, d_v) = jnp.split(z, split_points, axis=-1)

        y_gla = gla_branch(g_q, g_k, g_v, g_o, a_low, w_alpha_up[l], b_alpha[l], gla_norm_g[l])
        y_sc = sc_b * causal_dwconv(sc_c * sc_x, sc_conv_w[l])
        y_dil = dilated_branch(d_q, d_k, d_v, positions)

        br = jnp.stack([y_gla, y_sc, y_dil], axis=2)
        proj = jnp.einsum('bsgc,gcd->bsgd', br, w_branch[l])
        gates = jax.nn.sigmoid(h @ w_gate[l] + b_gate[l]).reshape(B, S, N_BRANCH, D_MODEL)
        merged = jnp.sum(gates * proj, axis=2)
        x = x + rmsnorm(merged @ w_mix_out[l], post_mix_g[l])

        h = rmsnorm(x, pre_ffn_g[l])
        gt = causal_dwconv(h @ w_ff_gate[l], ff_conv_w[l]) + ff_conv_b[l]
        y = (jax.nn.gelu(gt, approximate=True) * (h @ w_ff_up[l])) @ w_ff_down[l]
        x = x + rmsnorm(y, post_ffn_g[l])
    return x


def setup_inputs(seed=0):
    out = dict(first_inputs(seed))
    for name, value in second_inputs(seed + 1).items():
        if name != "x":
            out[name + "_2"] = value
    return out


def reference(
    x, c, ctx, c_ctx, w_ada, b_ada, g_norm_mix, g_norm_ffn, w_in, da_lambda, da_subln_g,
    sg_ln_g, sg_ln_b, sg_w, sg_b, na_rpb, w_branch, w_out, moe_w_group, moe_b_group,
    moe_w_router, moe_b_router, moe_w_gate, moe_w_up, moe_w_down, g_final, positions_2, w_in_2,
    w_alpha_up_2, b_alpha_2, gla_norm_g_2, sc_conv_w_2, w_gate_2, b_gate_2, w_branch_2,
    w_mix_out_2, pre_mix_g_2, post_mix_g_2, pre_ffn_g_2, post_ffn_g_2, w_ff_gate_2, w_ff_up_2,
    ff_conv_w_2, ff_conv_b_2, w_ff_down_2,
):
    x = first_block(
        x, c, ctx, c_ctx, w_ada, b_ada, g_norm_mix, g_norm_ffn, w_in, da_lambda, da_subln_g,
        sg_ln_g, sg_ln_b, sg_w, sg_b, na_rpb, w_branch, w_out, moe_w_group, moe_b_group,
        moe_w_router, moe_b_router, moe_w_gate, moe_w_up, moe_w_down, g_final,
    )
    return second_block(
        x, positions_2, w_in_2, w_alpha_up_2, b_alpha_2, gla_norm_g_2, sc_conv_w_2, w_gate_2,
        b_gate_2, w_branch_2, w_mix_out_2, pre_mix_g_2, post_mix_g_2, pre_ffn_g_2, post_ffn_g_2,
        w_ff_gate_2, w_ff_up_2, ff_conv_w_2, ff_conv_b_2, w_ff_down_2,
    )


_drawn_inputs = setup_inputs


def setup_inputs(seed=0):
    import zlib

    import numpy as np

    out = dict(_drawn_inputs(seed))
    spreads = {}
    factors = {'g_norm_mix': 3.59,
     'da_lambda': 3.603,
     'da_subln_g': 14.854,
     'sg_ln_g': 5.183,
     'sg_ln_b': 7.244,
     'sg_b': 5.221,
     'na_rpb': 8.0,
     'moe_b_group': 29.186,
     'moe_b_router': 18.612,
     'b_alpha_2': 2.969,
     'gla_norm_g_2': 6.129,
     'b_gate_2': 8.0,
     'post_mix_g_2': 3.427,
     'pre_ffn_g_2': 3.37,
     'post_ffn_g_2': 17.386,
     'ff_conv_b_2': 4.956,
     'g_norm_ffn': 4.681}
    for name, (base, spread) in spreads.items():
        noise = np.random.default_rng([zlib.crc32(name.encode()), seed]).standard_normal(out[name].shape)
        drawn = base * np.exp(spread * noise) if base else spread * noise
        out[name] = jnp.asarray(drawn.astype(out[name].dtype))
    for name, factor in factors.items():
        out[name] = (out[name] * factor).astype(out[name].dtype)
    return out
```

```python
import math
from contextlib import ExitStack, contextmanager

import numpy as np

import concourse.bass as bass
from concourse import mybir

F32 = mybir.dt.float32
I32 = mybir.dt.int32
ALU = mybir.AluOpType
ACT = mybir.ActivationFunctionType
X = mybir.AxisListType.X

P = 128
D = 1024
KD = D // P
SEQ, CTX = 256, 256
NT = (SEQ + CTX) // P
DEPTH = 2
GRID_W, NA_COLS, NA_ROWS = 64, 16, 8
ROWS = SEQ // GRID_W
EPS = 1e-6
NEG = -1e30
THETA = 10000.0
N_EXP, N_GRP, PER_GRP = 32, 4, 8
D_EXP = 512
CAP = P // 2
COLS = 512
SLOT = 4096
NSLOT = 4
NOLIMIT = 1 << 20
N_BLK = (SEQ + CTX) // CAP
HALF = D // 2
D_HALF = D_EXP // 2
MOE_AHEAD = 4
N_BR = 3
N_COND = P // 4

GLA_HEADS, GLA_CHUNK, GLA_RANK, GLA_TAU = 4, 16, 16, 16.0
DILATED = ((128, 1), (512, 4), (2048, 16))
D_FF = 2816
FF_TILES = D_FF // P
UP_CHUNKS = FF_TILES // 2
DOWN_K = 4
DOWN_CHUNKS = -(-FF_TILES // DOWN_K)


def shape_constants():
    at, parts = {}, []

    def put(name, a):
        a = np.asarray(a, np.float32)
        full = np.zeros((P, a.shape[1]), np.float32)
        full[: a.shape[0]] = a
        at[name] = (sum(p.shape[1] for p in parts), a.shape[1])
        parts.append(full)

    put("ident", np.eye(P))
    put("ones", np.ones((P, P)))
    put("minus_half", np.full((P, 32), -0.5))
    put("add_parts", np.tile(np.eye(P // 4)[:, :2], (4, 1)))
    put("earlier", np.triu(np.ones((P, P)), 1))
    q = 64 // 4
    rot = np.zeros((64, 64))
    for i in range(q):
        rot[i, q + i], rot[q + i, i] = -1, 1
        rot[2 * q + i, 3 * q + i], rot[3 * q + i, 2 * q + i] = -1, 1
    both = np.zeros((P, P))
    both[:64, :64] = both[64:, 64:] = rot
    put("rot_axial", both.T)
    t = np.arange(SEQ)
    inv = (np.float32(THETA) ** (-np.arange(q, dtype=np.float32) / np.float32(q))).astype(np.float32)
    ar = (t // GRID_W).astype(np.float32)[:, None] * inv
    ac = (t % GRID_W).astype(np.float32)[:, None] * inv
    ang = np.concatenate([ar, ar, ac, ac], axis=1)
    put("cos_axial", np.tile(np.cos(ang).T, (2, 1)))
    put("sin_axial", np.tile(np.sin(ang).T, (2, 1)))
    put("iota", np.tile(np.arange(N_EXP), (P, 1)))
    put("places", np.tile(np.arange(N_BLK * N_EXP), (P, 1)))
    ids = 2 * (np.arange(NT)[None, :, None] * P + np.arange(P)[:, None, None]) + np.arange(2)[None, None, :]
    put("half_row", 2 * ids.reshape(P, 2 * NT) - NOLIMIT)
    first = np.concatenate(parts, axis=1)
    kept = at["minus_half"][0] + at["minus_half"][1]
    parts = [first[:, :kept]]
    rot = np.zeros((P, P))
    for i in range(P // 2):
        rot[i, P // 2 + i], rot[P // 2 + i, i] = -1, 1
    put("rot_half", rot.T)
    tok = np.arange(P)
    put("chunk_causal", (tok[:, None] // GLA_CHUNK == tok[None, :] // GLA_CHUNK) & (tok[:, None] <= tok[None, :]))
    put("of_chunk", tok[:, None] // GLA_CHUNK == np.arange(P // GLA_CHUNK)[None, :])
    put("carry", np.tile(np.arange(SEQ) % GLA_CHUNK != 0, (P, 1)))
    inv = (np.float32(THETA) ** (-np.arange(0, P, 2, dtype=np.float32) / np.float32(P))).astype(np.float32)
    put("inv_freq", np.tile(inv, 2)[:, None])
    put("half_pi", np.full((P, 1), math.pi / 2))
    second = np.concatenate(parts, axis=1)[:, kept:]
    q, k = np.arange(SEQ)[:, None], np.arange(SEQ)[None, :]
    masks = [np.where((q >= k) & ((q - k) % dil == 0) & ((q - k) // dil <= win // dil), 0.0, NEG) for win, dil in DILATED]
    masks = np.stack(masks).reshape(len(DILATED), 2, P, SEQ).transpose(2, 0, 1, 3).astype(np.float32)
    return first, second, np.ascontiguousarray(masks), kept, at


CONST, CONST2, DIL_MASKS, KEPT, CONST_AT = shape_constants()


class Bank:

    def __init__(self, nc, ctx, name):
        self.t = ctx.enter_context(nc.psum_tensor(name, [P, 512], F32))
        self.full = ctx.enter_context(nc.semaphore(name + "_full"))
        self.free = ctx.enter_context(nc.semaphore(name + "_free"))
        self.fills = 0
        self.reads = 0
        self.seen = 0

    def fill(self):
        self.fills = self.fills + 1
        return 1

    def read(self):
        self.reads = self.reads + 1
        return 1

    def see(self):
        self.seen = self.seen + 1
        return self.seen


class Count:

    def __init__(self, nc, ctx, name):
        self.sem = ctx.enter_context(nc.semaphore(name))
        self.n = 0
        self.taken = {}

    def up(self, by=1):
        self.n = self.n + by
        return by

    def take(self, who, by=1):
        self.taken[who] = self.taken.get(who, 0) + by
        return self.taken[who]


class Turns:

    def __init__(self, *counted):
        self.counted = [(o, which, value_of(o, which), per) for o, which, per in counted]

    def turn(self, i):
        for o, which, base, per in self.counted:
            if which == "fills":
                o.fills = base + i * per
            elif which == "reads":
                o.reads = base + i * per
            elif which == "seen":
                o.seen = base + i * per
            else:
                o.n = base + i * per

    def done(self, n):
        self.turn(n)


def value_of(o, which):
    if which == "n":
        return o.n
    return o.fills if which == "fills" else o.reads if which == "reads" else o.seen


W_IN_BLOCKS = ("KA", "VA", "KC", "VC", "QA", "QC", "U", "V")
IN2_AT = {"qk": 0, "v": 512, "g": 1024, "sb": 1552, "sc": 2064, "sx": 2576}
IN2_AT.update({f"d{x}{i}": 3088 + 1536 * n + 512 * i for n, x in enumerate("qkv") for i in range(3)})
ALOW_AT = 1536
IN2_ORDER = ("qk", "v", "g", "sc", "sx", "sb", "dv0", "dv1", "dv2", "dq0", "dq1", "dq2", "dk0", "dk1", "dk2")
ADA_CHUNKS = 6 * D // COLS
ADA_FIRST = 2 * D // COLS
ADA_WITH = {"KA": (4, 5, 6), "QA": (7, 8, 9), "KC": (10, 11)}
MERGE_CHUNKS = D // P
OUT_CHUNKS = D // COLS


def chunk_order():
    order = []
    for l in range(DEPTH):
        order += [("ada", l, j) for j in range(ADA_FIRST)]
        for n in ("U", "V", "KA", "QA", "VA", "KC", "VC", "QC"):
            order += [("in", l, n)] + [("ada", l, j) for j in ADA_WITH.get(n, ())]
        order += [("bias", l, 0)]
        order += [("merge", l, d) for d in range(MERGE_CHUNKS)]
        order += [("out", l, j) for j in range(OUT_CHUNKS)]
        order += [("expert", l, 3 * e + r) for e in range(N_EXP) for r in range(3)]
    order += [("in2", 2, n) for n in IN2_ORDER]
    order += [("merge", 2, d) for d in range(MERGE_CHUNKS)]
    order += [("out", 2, j) for j in range(OUT_CHUNKS)]
    order += [("up", 2, j) for j in range(UP_CHUNKS)]
    order += [("down", 2, j) for j in range(DOWN_CHUNKS)]
    return order


ORDER = chunk_order()
PLACE = {c: i for i, c in enumerate(ORDER)}


def program(nc, t, out):
    ctx = ExitStack()
    with ctx:
        emit(nc, ctx, t, out)


def emit(nc, ctx, t, out):
    def tiles(l):
        return NT if l < DEPTH - 1 else SEQ // P

    def further(l):
        return 2 * tiles(l) * P // (CAP + 1)

    def sb(name, shape, dt=F32):
        return ctx.enter_context(nc.sbuf_tensor(name, shape, dt))

    def sem(name):
        return ctx.enter_context(nc.semaphore(name))

    def count(name):
        return Count(nc, ctx, name)

    ring = [sb(f"ring{i}", [P, SLOT]) for i in range(NSLOT)]
    ring_loaded = [sem(f"ring_loaded{i}") for i in range(NSLOT)]
    h = sb("h", [P, NT, D])
    xT = sb("xT", [P, KD, NT * P])
    heads = sb("heads", [P, 8192])
    values = sb("values", [P, 4096])
    branches = sb("branches", [P, 6144])
    work = sb("work", [P, 6144])
    tmp = sb("tmp", [P, 512])
    const = sb("const", [P, CONST.shape[1]])
    cols = sb("cols", [P, t["cols"].shape[1]])
    sgw = sb("sgw", [P, 4, P])
    wr = sb("wr", [P, DEPTH, KD, 36])
    rb = sb("rb", [1, DEPTH, 36])
    stat = sb("stat", [P, 192])
    table = sb("table", [P, N_BLK * N_EXP], I32)
    token_of = sb("token_of", [P, N_BLK * N_EXP], I32)
    further_list = sb("further_list", [1, DEPTH, 2 * further(0) + 1], I32)

    def C(name):
        a, n = CONST_AT[name]
        return const[:, a:a + n]

    def col(name, l=None):
        a, n = COLS_AT[name if l is None else f"{name}{l}"]
        return cols[:, a:a + n]

    ident, ones = C("ident"), C("ones")

    ada_rows = [branches[0:2, 1024 * i:1024 * (i + 1)] for i in (0, 1, 4, 5)]
    g2row = values[0:2, 2048:3072]
    qaT, kaT, qcT, kcT = [heads[:, 2048 * i:2048 * (i + 1)].rearrange("p (f n) -> p f n", f=4) for i in range(4)]
    gt1b, a2b, sh2b, gt2b = [heads[:, 2048 * i:2048 * (i + 1)].rearrange("p (s n) -> p s n", s=2) for i in range(4)]
    xhat = values[:, :].rearrange("p (t n) -> p t n", t=NT)
    va, vc = [values[:, 2048 * i:2048 * (i + 1)].rearrange("p (t n) -> p t n", t=NT) for i in range(2)]
    merged = values[:, :].rearrange("p (k n) -> p k n", k=KD)
    xn2 = xhat
    ybuf = values[:, :].rearrange("p (b n) -> p b n", b=2)
    ada_parts = heads[:, 0:ADA_FIRST * COLS]
    cond = work[:, 5632:5632 + KD * N_COND].rearrange("p (k s) -> p k s", k=KD)
    bias_rows = work[0:ADA_CHUNKS, 5120:5120 + COLS]
    ysT = branches[:, :].rearrange("p (i g n) -> p i g n", i=N_BR, g=4)
    lam_in = work[:, 0:DEPTH * 256].rearrange("p (l r n) -> p l r n", l=DEPTH, r=4)
    ln_rows = work[:, 4096:5120].rearrange("p (r n) -> p r n", r=2)
    u_sb = work[:, 0:1024].rearrange("p (b n) -> p b n", b=2)
    vv = work[:, 1024:2048].rearrange("p (b n) -> p b n", b=2)
    yb = work[:, 2048:4096].rearrange("p (t n) -> p t n", t=NT)
    probs = work[:, 0:2048].rearrange("p (b m n) -> p b m n", b=2, m=2)
    mix = work[:, 2048:3072].rearrange("p (b n) -> p b n", b=2)
    mixT = work[:, 3072:4096].rearrange("p (b k n) -> p b k n", b=2, k=4)
    o_rows = work[:, 4096:6144].rearrange("p (t n) -> p t n", t=NT)
    gate_s = work[:, 0:1024].rearrange("p (b n) -> p b n", b=2)
    part = work[:, 1024:2048].rearrange("p (b n) -> p b n", b=2)
    more = work[:, 2048:4096].rearrange("p (s n) -> p s n", s=NSLOT)
    xg = branches[:, 0:1024].rearrange("p (b n) -> p b n", b=2)
    xgT = branches[:, 2048:3072].rearrange("p (b k n) -> p b k n", b=2, k=KD // 2)
    hid = branches[:, 4096:4608].rearrange("p (b n) -> p b n", b=2)
    hidT = branches[:, 5120:5632].rearrange("p (b k n) -> p b k n", b=2, k=2)
    silu_s = work[:, 0:512].rearrange("p (b n) -> p b n", b=2)
    y_sb = work[:, 1024:2048].rearrange("p (b n) -> p b n", b=2)
    hot_slot = work[:, 0:1024].rearrange("p (q n) -> p q n", q=2 * NT)
    hot_place = work[:, 1024:3072].rearrange("p (q n) -> p q n", q=2 * NT)
    rt = work[:, 3072:6144]

    x2T = xT[:, 0:4, :].rearrange("p k n -> p (k n)").rearrange("p (k n) -> p k n", k=KD)
    spare = xT[:, 4:8, :].rearrange("p k n -> p (k n)")
    gqkT = spare[:, 0:1024].rearrange("p (f n) -> p f n", f=4)
    log_a = spare[:, 1024:1536].rearrange("p (f n) -> p f n", f=2)
    kin_rows = spare[:, 1536:2048].rearrange("p (t n) -> p t n", t=2)
    dqT, dkT = [heads[:, 3072 * i:3072 * (i + 1)].rearrange("p (f n) -> p f n", f=12) for i in range(2)]
    state = [h[:, 2:4, :].rearrange("p t n -> p (t n)").rearrange("p (c n) -> p c n", c=SEQ // GLA_CHUNK),
             heads[:, 6144:8192].rearrange("p (c n) -> p c n", c=SEQ // GLA_CHUNK)]
    dv = values[:, 0:3072].rearrange("p (t n) -> p t n", t=2)
    gv = values[:, 3072:4096].rearrange("p (t n) -> p t n", t=2)
    x2hat = values[:, 0:2048].rearrange("p (t n) -> p t n", t=2)
    ys2T = branches[:, 0:3072].rearrange("p (i g n) -> p i g n", i=N_BR, g=4)
    scoreT = ys2T[:, 2].rearrange("p g n -> p (g n)").rearrange("p (t h n) -> p t h n", t=2, h=4)
    cos2, sin2 = branches[:, 3072:3328], branches[:, 3328:3584]
    dil_mask = branches[:, 3584:5120].rearrange("p (d t n) -> p d t n", d=3, t=2)
    g2T = branches[:, 5120:6144].rearrange("p (f n) -> p f n", f=4)
    end_gap = work[:, 3584:4096].rearrange("p (f n) -> p f n", f=2)
    v_chunk = work[:, 0:4096].rearrange("p (c n) -> p c n", c=P // GLA_CHUNK)
    conv_in = work[:, 4096:4096 + 4 * (SEQ + 2)].rearrange("p (f n) -> p f n", f=4)
    qinT = work[:, 5128:5640].rearrange("p (f n) -> p f n", f=2)
    kinT = tmp[:, :].rearrange("p (f n) -> p f n", f=2)
    alowT = work[0:GLA_RANK, 5640:5896]
    o2T = work[:, 0:1024].rearrange("p (h n) -> p h n", h=4)
    o2sq = work[:, 1024:2048].rearrange("p (h n) -> p h n", h=4)
    o2r = stat[:, 156:164]
    pos_i = work[:, 0:256].bitcast(I32)
    ang, turns_of, sin_in, cos_in = [work[:, 256 * i:256 * (i + 1)] for i in range(1, 5)]
    d_sc = work[:, 0:1536].rearrange("p (b n) -> p b n", b=2)
    d_p = work[:, 1536:3072].rearrange("p (b n) -> p b n", b=2)
    d_pT = work[:, 3072:4608].rearrange("p (b k n) -> p b k n", b=2, k=6)
    y2 = work[:, 4096:6144].rearrange("p (t n) -> p t n", t=2)
    final_g = heads[:, 0:1024]
    hidden = heads[:, 0:FF_TILES * SEQ].rearrange("p (f n) -> p f n", f=FF_TILES)
    mix_g, ffn_g = heads[:, 5632:6656], heads[:, 6656:7680]
    gate_in = work[:, 0:2 * (SEQ + 2)].rearrange("p (b n) -> p b n", b=2)
    conved = work[:, 1024:1536].rearrange("p (b n) -> p b n", b=2)
    wr_flat = wr[:, :, :, :].rearrange("p l k n -> p (l k n)")
    w_alow = wr_flat[:, 0:KD * GLA_RANK].rearrange("p (k n) -> p k n", k=KD)
    w_alpha = wr_flat[0:GLA_RANK, 128:384]

    sq, rstd = stat[:, 0:4], stat[:, 4:8]
    mod_a, mod_b = [stat[:, 8 + 16 * i:24 + 16 * i].rearrange("p (k s) -> p k s", k=KD) for i in range(2)]
    neg_max = stat[:, 40:44]
    exp_sum = stat[:, 44:48]
    inv_sum = stat[:, 48:52]
    neglam = stat[:, 52:54]
    lam_s = stat[:, 54:58].rearrange("p (l m) -> p l m", l=DEPTH)
    bn6, bn2, ln_var, ln_r = stat[:, 58:64], stat[:, 64:66], stat[:, 66:67], stat[:, 67:68]
    head_sq, head_r = stat[:, 68:72], stat[:, 72:76]
    na_sum = stat[:, 76:92].rearrange("p (b h) -> p b h", b=2)
    na_inv = stat[:, 92:108].rearrange("p (b h) -> p b h", b=2)
    sub_g = stat[:, 108:110]
    decay = stat[:, 118:150].rearrange("p (f c) -> p f c", f=2)
    d_max, d_sum, d_inv = stat[:, 150:152], stat[:, 152:154], stat[:, 154:156]
    weight = stat[:, 110:118].rearrange("p (t k) -> p t k", t=NT)

    tmp_sq = work[:, 4096:5120]

    r_area, r_logits, r_gexp, r_e2 = [], [], [], []
    for l in range(DEPTH):
        nt = tiles(l)
        at, r = nt * N_EXP, {}
        for name, n in (("logits", 36), ("gexp", 4), ("e2", 1), ("gmax", 1), ("g1", 4), ("g2", 4), ("gidx", 1), ("ghot", 4),
                        ("sel", 32), ("w1", 32), ("w2", 32), ("m1", 1), ("i1", 1), ("hot1", 32), ("m2", 1), ("i2", 1),
                        ("hot2", 32), ("gsum", 1), ("den", 1), ("pos", 2), ("blk", 2)):
            r[name] = rt[:, at:at + nt * n].rearrange("p (t n) -> p t n", t=nt)
            at += nt * n
        r["cnt"] = rt[:, at:at + N_EXP]
        n_more = further(l)
        at = 1504
        for name, n in (("blocks", N_EXP), ("upto", N_EXP), ("gap", n_more * N_EXP), ("hot", n_more * N_EXP),
                        ("val", n_more * N_EXP)):
            r["x_" + name] = rt[0:1, at:at + n]
            at += n
        r["x_pair"] = rt[0:1, 1410:1410 + 2 * n_more]
        r["x_list"] = further_list[:, l, 0:2 * n_more + 1]
        r["x_ids"] = rt[:, 1400:1402].bitcast(I32)
        r_area.append(r)
        r_logits.append(r["logits"])
        r_gexp.append(r["gexp"])
        r_e2.append(r["e2"])

    A = [Bank(nc, ctx, f"act_bank{i}") for i in range(2)]
    S = [Bank(nc, ctx, f"score_bank{i}") for i in range(2)]
    V = [Bank(nc, ctx, f"vec_bank{i}") for i in range(4)]

    mod_rows = [nc.dram_tensor(f"mod_rows{l}", (2, 4, D), F32).ap() for l in range(DEPTH)]
    x_rows = [nc.dram_tensor(f"x_rows{l}", (NT * P, D), F32).ap() for l in range(DEPTH)]
    y_rows = [nc.dram_tensor(f"y_rows{l}", (NT * P * 2, D), F32).ap() for l in range(DEPTH)]

    first_loaded = sem("first_loaded")
    setup = sem("setup_loaded")
    SETUP = 5
    more_loaded = [sem(f"more_loaded{i}") for i in range(NSLOT)]
    silu_done, cond_zero = count("silu_done"), count("cond_zero")
    lam_prod, lam_exp, lam_done = count("lam_prod"), count("lam_exp"), count("lam_done")
    bias_in = sem("bias_in")
    rows_in = [sem(f"rows_in{l}") for l in range(DEPTH)]
    sq_done = count("sq_done")
    pow_in, pow_out = count("pow_in"), count("pow_out")
    xhat_done = count("xhat_done")
    modrow_done, modrow_stored = count("modrow_done"), sem("modrow_stored")
    vv_done = count("vv_done")
    rope_done = count("rope_done")
    neg_max_done = count("neg_max_done")
    mix_done = count("mix_done")
    p_done = count("p_done")
    o_done = count("o_done")
    merge_done = count("merge_done")
    h_done = count("h_done")
    mods_in = [sem(f"mods_in{l}") for l in range(DEPTH)]
    xn2_done = count("xn2_done")
    x_stored = [sem(f"x_stored{l}") for l in range(DEPTH)]
    route_exp_in, route_exp_out = count("route_exp_in"), count("route_exp_out")
    picked = count("picked")
    hot_done = count("hot_done")
    token_done = count("token_done")
    gathered = [sem(f"gathered{b}") for b in range(2)]
    scattered = [sem(f"scattered{b}") for b in range(2)]
    y_half_done = count("y_half_done")
    y_in = [sem(f"y_in{b}") for b in range(2)]
    block2_in = [sem(f"block2_in{i}") for i in range(3)]
    final_done = count("final_done")
    alow_exp_in, alow_exp_out = count("alow_exp_in"), count("alow_exp_out")
    decay_in, decay_out = count("decay_in"), count("decay_out")
    gla_cols = count("gla_cols")
    v_chunk_done = count("v_chunk_done")
    rope_in, rope_table = count("rope_in"), count("rope_table")
    d_rope_done = count("d_rope_done")
    d_max_done, d_exp_done, d_p_done = count("d_max_done"), count("d_exp_done"), count("d_p_done")
    down_used = count("down_used")
    o2sq_done = count("o2sq_done")
    y_gla_done = count("y_gla_done")
    conv_done, gelu_done = count("conv_done"), count("gelu_done")
    x_done = count("x_done")
    dve_step = count("dve_step")
    out_stored = sem("out_stored")
    names = ("list", "weights", "rows", "pe", "act", "dve", "index", "sent", "passed")
    xb = [{n: sem(f"further_{n}{l}") for n in names} for l in range(DEPTH)]
    mark = {}

    def h_done_mix(l):
        return sum(3 * tiles(k) for k in range(l)) + 2 * tiles(l)

    def h_end(l):
        return h_done_mix(l) + tiles(l)

    o2r_power = sum(2 + 2 * tiles(l) for l in range(DEPTH)) + 2 + 1

    def at_bank(b):
        return (b.full, b.fills)

    def let_go(b):
        return (b.free, b.fills)

    @contextmanager
    def further_blocks(eng, l):
        eng.wait_ge(xb[l]["list"], 1)
        n = eng.value_load(r_area[l]["x_list"][:, 0:1], min_val=0, max_val=further(l))
        with eng.Fori(0, further(l)) as j:
            with eng.If(j < n):
                yield j

    block = ctx.enter_context(nc.Block())

    @block.tensor
    def _(pe):
        def slot_of(c):
            n = PLACE[c]
            pe.wait_ge(ring_loaded[n % NSLOT], 16 * (n // NSLOT + 1))
            return ring[n % NSLOT]

        def used(c, b):
            mark[("used",) + c] = at_bank(b)

        def emptied(*banks):
            for b in banks:
                pe.wait_ge(b.free, b.fills)

        def bias_of(j):
            return ident[0:ADA_CHUNKS, j:j + 1].to_broadcast([ADA_CHUNKS, 2])

        def ada_part(l, j, b):
            w = slot_of(("ada", l, j))
            pe.wait_ge(b.free, b.fills)
            for k in range(KD):
                g = k % 4
                mm = pe.matmul(b.t[g * N_COND:(g + 1) * N_COND, :], cond[:, k, :], w[:, k * COLS:(k + 1) * COLS],
                               start=(k < 4), stop=(k >= 4))
            mm.then_inc(b.full, b.fill())
            used(("ada", l, j), b)
            mark["ada_part", l, j] = let_go(b)

        def whole_rows(l, j):
            b = S[1]
            pe.wait_ge(*mark["ada_part", l, j])
            pe.wait_ge(b.free, b.fills)
            pe.matmul(b.t[0:2, :], C("add_parts"), tmp[:, :], start=True, stop=False)
            pe.matmul(b.t[0:2, :], bias_of(j), bias_rows, start=False, stop=True).then_inc(b.full, b.fill())
            mark["ada", l] = let_go(b)

        def modulation(l):
            pe.wait_ge(silu_done.sem, l + 1)
            pe.wait_ge(cond_zero.sem, l + 1)
            for j in range(ADA_FIRST):
                ada_part(l, j, A[j % 2])
            emptied(A[0], A[1])
            pe.wait_ge(bias_in, 16 * (l + 1))
            b = V[0]
            pe.wait_ge(b.free, b.fills)
            for q in range(2 * KD):
                o = b.t[:, 2 * q:2 * q + 2]
                c = q * P % COLS
                pe.matmul(o, ada_parts[:, q * P:(q + 1) * P], C("add_parts"), start=True, stop=False)
                mm = pe.matmul(o, bias_rows[:, c:c + P], bias_of(q * P // COLS), start=False, stop=True)
            mm.then_inc(b.full, b.fill())
            mark["mod", l] = let_go(b)

        def norm_columns(l):
            pe.wait_ge(xhat_done.sem, 4 * (l + 1))
            for f in range(KD):
                for s in range(2):
                    b = (A if f % 2 == 0 else V)[s]
                    pe.wait_ge(b.free, b.fills)
                    for j in range(2):
                        mm = pe.transpose(b.t[:, j * P:(j + 1) * P], xhat[:, 2 * s + j, f * P:(f + 1) * P], ident)
                    mm.then_inc(b.full, b.fill())
            emptied(A[0], A[1], V[0], V[1])
            mark["normed", l] = at_bank(V[1])

        def rows_group(b, w, c0, tile, n=COLS):
            for k in range(KD):
                mm = pe.matmul(b.t[:, 0:n], xT[:, k, tile * P:(tile + 1) * P], w[:, k * COLS + c0:k * COLS + c0 + n],
                               start=(k == 0), stop=(k == KD - 1))
            return mm

        def columns_chunk(c, n):
            w = slot_of(c)
            late = ADA_WITH.get(c[2], ())
            for f in range(4):
                if 0 < f <= len(late):
                    if f >= 2:
                        whole_rows(c[1], late[f - 2])
                    ada_part(c[1], late[f - 1], S[0])
                b = A[f % 2]
                pe.wait_ge(b.free, b.fills)
                for k in range(KD):
                    mm = pe.matmul(b.t[:, 0:n], w[:, k * COLS + f * P:k * COLS + (f + 1) * P], xT[:, k, 0:n],
                                   start=(k == 0), stop=(k == KD - 1))
                mm.then_inc(b.full, b.fill())
            used(c, A[1])
            if late:
                whole_rows(c[1], late[-1])

        def rows_chunk(c):
            w = slot_of(c)
            for tile in range(NT):
                b = A[tile % 2]
                pe.wait_ge(b.free, b.fills)
                rows_group(b, w, 0, tile).then_inc(b.full, b.fill())
            used(c, A[(NT - 1) % 2])

        def turn_rows(src, tile):
            b = A[tile % 2]
            pe.wait_ge(b.free, b.fills)
            for g in range(4):
                mm = pe.transpose(b.t[:, g * P:(g + 1) * P], src[:, tile, g * P:(g + 1) * P], ident)
            mm.then_inc(b.full, b.fill())

        def projections(l):
            nt = tiles(l)
            wu, wv = slot_of(("in", l, "U")), slot_of(("in", l, "V"))

            def gate_tile(tile):
                b = V[tile % 2]
                pe.wait_ge(vv_done.sem, vv_done.take("pe"))
                pe.wait_ge(b.free, b.fills)
                for g in range(4):
                    mm = pe.matmul(b.t[:, g * P:(g + 1) * P], sgw[:, g, :], vv[:, tile % 2, g * P:(g + 1) * P],
                                   start=True, stop=True)
                mm.then_inc(b.full, b.fill())
                mark["yb", l, tile] = let_go(b)

            for tile in range(nt):
                for b, w, what in ((A[0], wu, "u"), (A[1], wv, "v")):
                    pe.wait_ge(b.free, b.fills)
                    rows_group(b, w, 0, tile).then_inc(b.full, b.fill())
                    mark[what, l, tile] = let_go(b)
                if tile >= 1:
                    gate_tile(tile - 1)
            used(("in", l, "U"), A[0])
            used(("in", l, "V"), A[1])
            gate_tile(nt - 1)
            columns_chunk(("in", l, "KA"), NT * P)
            columns_chunk(("in", l, "QA"), nt * P)
            mark["qk", l] = (let_go(A[0]), let_go(A[1]))
            for tile in range(nt):
                pe.wait_ge(*mark["yb", l, tile])
                turn_rows(yb, tile)
            emptied(A[0], A[1])
            for i in range(8):
                b = V[i % 2]
                pe.wait_ge(b.free, b.fills)
                pe.matmul(b.t[:, 0:SEQ], C("rot_axial"), (kaT if i < 4 else qaT)[:, i % 4, 0:SEQ],
                          start=True, stop=True).then_inc(b.full, b.fill())
            rows_chunk(("in", l, "VA"))
            columns_chunk(("in", l, "KC"), NT * P)
            rows_chunk(("in", l, "VC"))
            columns_chunk(("in", l, "QC"), nt * P)
            emptied(A[0], A[1])

        def attend(items, scores, weigh, value, ahead):
            for i in range(ahead):
                scores(i)
            for i in range(len(items) + 1):
                if i + ahead < len(items):
                    scores(i + ahead)
                if i < len(items):
                    weigh(i)
                if i >= 1:
                    value(i - 1)

        def key_tiles(tile):
            return range(NT) if tile < 2 else range(2, NT)

        def differential(l):
            items = [(tile, hd) for tile in range(tiles(l)) for hd in range(4)]
            pe.wait_ge(rope_done.sem, 8 * (l + 1))

            def scores(i):
                tile, hd = items[i]
                kt = key_tiles(tile)
                for m in range(2):
                    pe.wait_ge(S[m].free, S[m].fills)
                    pe.matmul(S[m].t[:, 0:len(kt) * P], qaT[64 * m:64 * m + 64, hd, tile * P:(tile + 1) * P],
                              kaT[64 * m:64 * m + 64, hd, kt[0] * P:NT * P], start=True,
                              stop=True).then_inc(S[m].full, S[m].fill())

            def weigh(i):
                tile, hd = items[i]
                b = A[i % 2]
                pe.wait_ge(mix_done.sem, mix_done.take("pe"))
                pe.wait_ge(b.free, b.fills)
                for j in range(len(key_tiles(tile))):
                    mm = pe.transpose(b.t[:, j * P:(j + 1) * P], mix[:, i % 2, j * P:(j + 1) * P], ident)
                mm.then_inc(b.full, b.fill())
                mark["mixed", l, i] = at_bank(b)
                mark["mixT", l, i] = let_go(b)

            def value(i):
                tile, hd = items[i]
                kt = key_tiles(tile)
                o = V[tile % 2]
                if hd == 0:
                    pe.wait_ge(o.free, o.fills)
                pe.wait_ge(*mark["mixT", l, i])
                for j, k in enumerate(kt):
                    mm = pe.matmul(o.t[:, hd * P:(hd + 1) * P], mixT[:, i % 2, j, :], va[:, k, hd * P:(hd + 1) * P],
                                   start=(j == 0), stop=(j == len(kt) - 1))
                if hd == 3:
                    mm.then_inc(o.full, o.fill())

            attend(items, scores, weigh, value, 1)
            for tile in range(tiles(l)):
                pe.wait_ge(o_done.sem, o_done.take("pe"))
                turn_rows(o_rows, tile)
            mark["da_turned", l] = (at_bank(A[0]), at_bank(A[1]))

        def neighbourhood(l):
            items = [(tile, hd) for tile in range(tiles(l)) for hd in range(8)]

            def scores(i):
                tile, hd = items[i]
                b = V[i % 2] if tile < 2 else S[i % 2]
                kt = key_tiles(tile)
                r = 64 * (hd % 2)
                pe.wait_ge(b.free, b.fills)
                pe.matmul(b.t[:, 0:len(kt) * P], qcT[r:r + 64, hd // 2, tile * P:(tile + 1) * P],
                          kcT[r:r + 64, hd // 2, kt[0] * P:NT * P], start=True, stop=True).then_inc(b.full, b.fill())
                mark["s_exp", l, i] = let_go(b)

            def weigh(i):
                tile, hd = items[i]
                b = A[i % 2]
                if tile < 2:
                    pe.wait_ge(p_done.sem, p_done.take("pe"))
                else:
                    pe.wait_ge(*mark["s_exp", l, i])
                pe.wait_ge(b.free, b.fills)
                for j in range(len(key_tiles(tile))):
                    mm = pe.transpose(b.t[:, j * P:(j + 1) * P], probs[:, i % 2, 0, j * P:(j + 1) * P], ident)
                mm.then_inc(b.full, b.fill())
                mark["turned", l, i] = at_bank(b)
                mark["pT", l, i] = let_go(b)

            def value(i):
                tile, hd = items[i]
                kt = key_tiles(tile)
                o = V[2 + tile % 2]
                if hd == 0:
                    pe.wait_ge(o.free, o.fills)
                pe.wait_ge(*mark["pT", l, i])
                for j, k in enumerate(kt):
                    mm = pe.matmul(o.t[:, hd * 64:(hd + 1) * 64], mixT[:, i % 2, j, :], vc[:, k, hd * 64:(hd + 1) * 64],
                                   start=(j == 0), stop=(j == len(kt) - 1))
                if hd == 7:
                    mm.then_inc(o.full, o.fill())
                    mark["o", l, tile] = let_go(o)

            attend(items, scores, weigh, value, 2)
            mark["used", "bias", l, 0] = mark["turned", l, 15]
            for tile in range(tiles(l)):
                pe.wait_ge(*mark["o", l, tile])
                turn_rows(o_rows, tile)
            emptied(A[0], A[1])
            mark["attended", l] = at_bank(A[(tiles(l) - 1) % 2])

        def merge(l, xs=xT, ys=ysT):
            n = tiles(l) * P
            mark["merge", l] = (A[0].fills, A[1].fills, V[0].fills, V[1].fills)
            place = PLACE["merge", l, 0]
            turns = Turns(*[(b, "fills", 6) for b in (A[0], A[1], V[0], V[1])])
            with pe.Fori(0, MERGE_CHUNKS // NSLOT) as i:
                turns.turn(i)
                for dd in range(NSLOT):
                    s = (place + dd) % NSLOT
                    pe.wait_ge(ring_loaded[s], 16 * ((place + dd) // NSLOT + 1) + 16 * i)
                    pe.wait_ge(more_loaded[s], 16 * (MERGE_CHUNKS // NSLOT * l + 1) + 16 * i)
                    w = ring[s]
                    for br in range(N_BR):
                        j = N_BR * dd + br
                        g, y = A[j % 2], V[j % 2]
                        pe.wait_ge(g.free, g.fills)
                        for k in range(KD):
                            c0 = (br * KD + k) * P
                            mm = pe.matmul(g.t[:, 0:n], w[:, c0:c0 + P], xs[:, k, 0:n], start=(k == 0), stop=(k == KD - 1))
                        mm.then_inc(g.full, g.fill())
                        pe.wait_ge(y.free, y.fills)
                        for k in range(4):
                            c0 = (N_BR * KD + br * 4 + k) * P
                            wk = w[:, c0:c0 + P] if br < 2 else more[:, s, k * P:(k + 1) * P]
                            mm = pe.matmul(y.t[:, 0:n], wk, ys[:, br, k, 0:n], start=(k == 0), stop=(k == 3))
                        mm.then_inc(y.full, y.fill())
            turns.done(MERGE_CHUNKS // NSLOT)
            pe.wait_ge(merge_done.sem, 2 * MERGE_CHUNKS * (l + 1))
            for c in range(OUT_CHUNKS):
                w = slot_of(("out", l, c))
                for tile in range(tiles(l)):
                    b = V[2 + tile % 2]
                    pe.wait_ge(b.free, b.fills)
                    for k in range(KD):
                        mm = pe.matmul(b.t[:, :], merged[:, k, tile * P:(tile + 1) * P], w[:, k * COLS:(k + 1) * COLS],
                                       start=(k == 0), stop=(k == KD - 1))
                    mm.then_inc(b.full, b.fill())
                used(("out", l, c), V[2 + (tiles(l) - 1) % 2])

        def route(l):
            nt = tiles(l)
            for tile in range(nt):
                pe.wait_ge(xn2_done.sem, xn2_done.take("pe"))
                for q in range(2):
                    b = A[q]
                    pe.wait_ge(b.free, b.fills)
                    for f in range(4):
                        mm = pe.transpose(b.t[:, f * P:(f + 1) * P], xn2[:, tile, (4 * q + f) * P:(4 * q + f + 1) * P], ident)
                    mm.then_inc(b.full, b.fill())
            emptied(A[0], A[1])
            b = V[0]
            pe.wait_ge(b.free, b.fills)
            for tile in range(nt):
                o = b.t[:, tile * 36:(tile + 1) * 36]
                for k in range(KD):
                    pe.matmul(o, xT[:, k, tile * P:(tile + 1) * P], wr[:, l, k, :], start=(k == 0), stop=False)
                mm = pe.matmul(o, ones[0:1, :], rb[0:1, l, :], start=False, stop=True)
            mm.then_inc(b.full, b.fill())
            pe.wait_ge(picked.sem, l + 1)
            b = V[1]
            pe.wait_ge(b.free, b.fills)
            pick = rt[:, 0:nt * N_EXP].rearrange("p (t e) -> p t e", t=nt)
            for tile in range(nt):
                for j in range(tile + 1):
                    mm = pe.matmul(b.t[:, tile * N_EXP:(tile + 1) * N_EXP], ones if j < tile else C("earlier"),
                                   pick[:, j, :], start=(j == 0), stop=(j == tile))
            for j in range(nt):
                mm = pe.matmul(b.t[:, NT * N_EXP:(NT + 1) * N_EXP], ones, pick[:, j, :], start=(j == 0), stop=(j == nt - 1))
            mm.then_inc(b.full, b.fill())
            b = V[2]
            pe.wait_ge(b.free, b.fills)
            for q in range(2 * nt):
                pe.wait_ge(hot_done.sem, hot_done.take("pe"))
                mm = pe.matmul(b.t[:, 0:N_BLK * N_EXP], hot_slot[:, q, :], hot_place[:, q, :], start=(q == 0), stop=(q == 2 * nt - 1))
            mm.then_inc(b.full, b.fill())

        def turn_half_rows(src, o, n):
            for k in range(n):
                mm = pe.transpose(o.t[:, k * P:(k + 1) * P], src[:, k * P:(k + 1) * P], ident)
            return mm

        def up_product(o, b, w):
            for k in range(KD):
                half, c = k // (KD // 2), k % (KD // 2)
                for g in range(2):
                    c0 = k * COLS + g * D_HALF
                    mm = pe.matmul(o.t[g * CAP:(g + 1) * CAP, 0:D_HALF], xgT[:, b, c, half * CAP:(half + 1) * CAP],
                                   w[:, c0:c0 + D_HALF], start=(k == 0), stop=(k == KD - 1))
            return mm

        def down_product(o, b, w):
            for k in range(4):
                half, c = k // 2, k % 2
                for g in range(2):
                    c0 = k * D + g * HALF
                    mm = pe.matmul(o.t[g * CAP:(g + 1) * CAP, :], hidT[:, b, c, half * CAP:(half + 1) * CAP],
                                   w[:, c0:c0 + HALF], start=(k == 0), stop=(k == 3))
            return mm

        def turn_tokens(b, n):
            pe.wait_ge(gathered[b], 16 * n)
            pe.wait_ge(A[1].free, A[1].fills)
            turn_half_rows(xg[:, b, :], A[1], 4).then_inc(A[1].full, A[1].fill())

        def expert(l, q, loaded, gathers):
            b = q % 2
            c = PLACE["expert", l, 0] + 3 * q
            s = [(c + r) % NSLOT for r in range(3)]
            pe.wait_ge(A[1].free, A[1].fills)
            for r, o in ((0, S[b]), (1, V[b])):
                pe.wait_ge(ring_loaded[s[r]], loaded(r))
                pe.wait_ge(o.free, o.fills)
                up_product(o, b, ring[s[r]]).then_inc(o.full, o.fill())
            if gathers is not None:
                turn_tokens(1 - b, gathers)
            pe.wait_ge(V[b].free, V[b].fills)
            pe.wait_ge(A[0].free, A[0].fills)
            turn_half_rows(hid[:, b, :], A[0], 2).then_inc(A[0].full, A[0].fill())
            o = V[2 + b]
            pe.wait_ge(ring_loaded[s[2]], loaded(2))
            pe.wait_ge(o.free, o.fills)
            pe.wait_ge(A[0].free, A[0].fills)
            down_product(o, b, ring[s[2]]).then_inc(o.full, o.fill())

        def experts(l):
            g0 = N_EXP // 2 * l
            n_turn = N_EXP // MOE_AHEAD
            c = PLACE["expert", l, 0]

            def loads(q, r, i):
                return 16 * ((c + 3 * q + r) // NSLOT + 1) + 48 * i

            turn_tokens(0, g0 + 1)
            mark["moe", l] = {"S": [b.fills for b in S], "V": [b.fills for b in V], "A": [b.fills for b in A]}
            turns = Turns(*[(b, "fills", 2) for b in S + V], (A[0], "fills", 4), (A[1], "fills", 4))
            with pe.Fori(0, n_turn - 1) as i:
                turns.turn(i)
                for q in range(MOE_AHEAD):
                    expert(l, q, lambda r: loads(q, r, i), g0 + (q + 1) // 2 + 1 + 2 * i)
            turns.done(n_turn - 1)
            for q in range(MOE_AHEAD):
                last = n_turn - 1
                expert(l, q, lambda r: loads(q, r, last),
                       g0 + (q + 1) // 2 + 1 + 2 * last if q < MOE_AHEAD - 1 else None)
            mark["moe_end", l] = at_bank(V[3])
            with further_blocks(pe, l) as j:
                s = xb[l]
                emptied(*A, *S, *V)
                pe.wait_ge(s["rows"], 16 * j + 16)
                turn_half_rows(xg[:, 0, :], A[1], 4).then_inc(s["pe"], 1)
                pe.wait_ge(s["act"], 3 * j + 1)
                pe.wait_ge(s["weights"], 48 * j + 48)
                up_product(S[0], 0, ring[0])
                up_product(V[0], 0, ring[1]).then_inc(s["pe"], 1)
                pe.wait_ge(s["dve"], 2 * j + 1)
                turn_half_rows(hid[:, 0, :], A[0], 2).then_inc(s["pe"], 1)
                pe.wait_ge(s["act"], 3 * j + 3)
                down_product(V[2], 0, ring[2]).then_inc(s["pe"], 1)
                pe.wait_ge(s["dve"], 2 * j + 2)

        def norm2_columns(n):
            pe.wait_ge(xhat_done.sem, 4 * DEPTH + 2 * n)
            for f in range(KD):
                b = A[f % 2]
                pe.wait_ge(b.free, b.fills)
                for j in range(2):
                    mm = pe.transpose(b.t[:, j * P:(j + 1) * P], x2hat[:, j, f * P:(f + 1) * P], ident)
                mm.then_inc(b.full, b.fill())
            emptied(A[0], A[1])

        def columns2(name, banks):
            w = slot_of(("in2", 2, name))
            for f in range(4):
                b = banks[f % 2]
                pe.wait_ge(b.free, b.fills)
                for k in range(KD):
                    mm = pe.matmul(b.t[:, 0:SEQ], w[:, k * COLS + f * P:k * COLS + (f + 1) * P], x2T[:, k, :],
                                   start=(k == 0), stop=(k == KD - 1))
                mm.then_inc(b.full, b.fill())
            used(("in2", 2, name), banks[1])

        def rows2(name):
            w = slot_of(("in2", 2, name))
            for tile in range(2):
                b = A[tile]
                pe.wait_ge(b.free, b.fills)
                for k in range(KD):
                    mm = pe.matmul(b.t[:, :], x2T[:, k, tile * P:(tile + 1) * P], w[:, k * COLS:(k + 1) * COLS],
                                   start=(k == 0), stop=(k == KD - 1))
                mm.then_inc(b.full, b.fill())
            used(("in2", 2, name), A[1])

        def linear_attention_in():
            columns2("qk", A)
            mark["gqk"] = (let_go(A[0]), let_go(A[1]))
            pe.wait_ge(block2_in[0], 16 * 4)
            b = A[0]
            pe.wait_ge(b.free, b.fills)
            for k in range(KD):
                mm = pe.matmul(b.t[0:GLA_RANK, 0:SEQ], w_alow[:, k, :], x2T[:, k, :], start=(k == 0), stop=(k == KD - 1))
            mm.then_inc(b.full, b.fill())
            rows2("v")
            mark["gv"] = (let_go(A[0]), let_go(A[1]))
            emptied(A[0])
            b = V[0]
            pe.wait_ge(b.free, b.fills)
            for f in range(2):
                mm = pe.matmul(b.t[:, f * SEQ:(f + 1) * SEQ], w_alpha[:, f * P:(f + 1) * P], alowT, start=True, stop=True)
            mm.then_inc(b.full, b.fill())
            columns2("g", A)

        def short_conv():
            columns2("sc", A)
            mark["sc"] = (let_go(A[0]), let_go(A[1]))
            columns2("sx", V[2:])
            columns2("sb", V[2:])

        def linear_attention():
            pe.wait_ge(gla_cols.sem, 4)
            b = A[0]
            pe.wait_ge(b.free, b.fills)
            for tile in range(2):
                for f in range(2):
                    q = (2 * tile + f) * P
                    mm = pe.transpose(b.t[:, q:q + P], kinT[:, f, tile * P:(tile + 1) * P], ident)
            mm.then_inc(b.full, b.fill())
            for m in range(2):
                b = V[m]
                r = 64 * m
                pe.wait_ge(b.free, b.fills)
                for tile in range(2):
                    c = slice(tile * P, (tile + 1) * P)
                    for f in range(2):
                        c0 = (2 * tile + f) * P
                        mm = pe.matmul(b.t[:, c0:c0 + P], gqkT[r:r + 64, 2 + f, c], gqkT[r:r + 64, f, c], start=True, stop=True)
                mm.then_inc(b.full, b.fill())
                mark["scoreT", m] = let_go(b)
            emptied(A[0])
            n = 0
            for tile in range(2):
                pe.wait_ge(v_chunk_done.sem, 8 * (tile + 1))
                for half in range(2):
                    for f in range(2):
                        b = V[n % 2]
                        n += 1
                        pe.wait_ge(b.free, b.fills)
                        for hd in (2 * f, 2 * f + 1):
                            r = 64 * (hd % 2)
                            mm = pe.matmul(b.t[r:r + 64, :], kin_rows[:, tile, hd * 64:(hd + 1) * 64],
                                           v_chunk[:, 4 * half:4 * half + 4, hd * P:(hd + 1) * P], start=True, stop=True)
                        mm.then_inc(b.full, b.fill())
                mark["v_chunk", tile] = (at_bank(V[0]), at_bank(V[1]))
            mark["state"] = (let_go(V[0]), let_go(V[1]))

        def linear_attention_out():
            for w in (*mark["state"], mark["scoreT", 0], mark["scoreT", 1]):
                pe.wait_ge(*w)
            per = P // GLA_CHUNK
            for m in range(2):
                b = V[2 + m]
                r = 64 * m
                pe.wait_ge(b.free, b.fills)
                for f in range(2):
                    hd = 2 * f + m
                    for tile in range(2):
                        c0 = f * SEQ + tile * P
                        pe.matmul(b.t[:, c0:c0 + P], gv[:, tile, hd * P:(hd + 1) * P], scoreT[:, tile, hd, :],
                                  start=True, stop=False)
                        for j in range(per):
                            n = tile * per + j
                            if n >= 1:
                                mm = pe.matmul(b.t[:, c0 + j * GLA_CHUNK:c0 + (j + 1) * GLA_CHUNK], state[f][r:r + 64, n - 1, :],
                                               qinT[r:r + 64, f, n * GLA_CHUNK:(n + 1) * GLA_CHUNK], start=False,
                                               stop=(j == per - 1))
                mm.then_inc(b.full, b.fill())
            pe.wait_ge(o2sq_done.sem, 1)
            b = V[0]
            pe.wait_ge(b.free, b.fills)
            for q in range(2 * GLA_HEADS):
                mm = pe.matmul(b.t[:, q:q + 1], o2sq[:, q // 2, q % 2 * P:(q % 2 + 1) * P], ones[:, 0:1], start=True, stop=True)
            mm.then_inc(b.full, b.fill())
            pe.wait_ge(pow_out.sem, o2r_power)
            for half in range(2):
                b = V[half]
                pe.wait_ge(b.free, b.fills)
                for q in range(4):
                    mm = pe.matmul(b.t[:, q * P:(q + 1) * P], o2r[:, 4 * half + q:4 * half + q + 1].to_broadcast([P, P]), ident,
                                   start=True, stop=True)
                mm.then_inc(b.full, b.fill())

        def dilated_in():
            for i in range(3):
                rows2(f"dv{i}")
            mark["dv"] = (let_go(A[0]), let_go(A[1]))
            for x in "qk":
                for i in range(3):
                    columns2(f"d{x}{i}", A)
                    emptied(A[0], A[1])
                    rotate(x, i)

        def rotate(x, i):
            src = dqT if x == "q" else dkT
            mark["d_in", x, i] = (let_go(A[0]), let_go(A[1]))
            for j in range(2):
                b = V[j]
                pe.wait_ge(b.free, b.fills)
                for f in range(2):
                    mm = pe.matmul(b.t[:, f * SEQ:(f + 1) * SEQ], C("rot_half"), src[:, 4 * i + 2 * j + f, :],
                                   start=True, stop=True)
                mm.then_inc(b.full, b.fill())

        def dilated():
            items = [(tile, hd) for tile in range(2) for hd in range(4)]
            pe.wait_ge(d_rope_done.sem, 12)

            def scores(i):
                tile, hd = items[i]
                n = (tile + 1) * P
                for g in range(3):
                    b = V[2 * (i % 2) + (g * n) // 512]
                    c0 = (g * n) % 512
                    if c0 == 0:
                        pe.wait_ge(b.free, b.fills)
                    mm = pe.matmul(b.t[:, c0:c0 + n], dqT[:, 4 * g + hd, tile * P:(tile + 1) * P], dkT[:, 4 * g + hd, 0:n],
                                   start=True, stop=True)
                    if g == 2 or (g + 1) * n % 512 == 0:
                        mm.then_inc(b.full, b.fill())

            def weigh(i):
                tile, hd = items[i]
                n = 3 * (tile + 1)
                pe.wait_ge(d_p_done.sem, i + 1)
                for j in range(n):
                    b = A[j // 4]
                    if j % 4 == 0:
                        pe.wait_ge(b.free, b.fills)
                    mm = pe.transpose(b.t[:, j % 4 * P:(j % 4 + 1) * P], d_p[:, i % 2, j * P:(j + 1) * P], ident)
                    if j % 4 == 3 or j == n - 1:
                        mm.then_inc(b.full, b.fill())
                mark["d_turned", i] = at_bank(A[(n - 1) // 4])
                mark["d_pT", i] = (let_go(A[0]), let_go(A[1]))

            def value(i):
                tile, hd = items[i]
                n = tile + 1
                b = S[i % 2]
                for w in mark["d_pT", i]:
                    pe.wait_ge(*w)
                pe.wait_ge(b.free, b.fills)
                for j in range(3 * n):
                    g, k = j // n, j % n
                    mm = pe.matmul(b.t[:, 0:P], dv[:, k, (4 * g + hd) * P:(4 * g + hd + 1) * P], d_pT[:, i % 2, j, :],
                                   start=(j == 0), stop=(j == 3 * n - 1))
                mm.then_inc(b.full, b.fill())

            attend(items, scores, weigh, value, 2)
            emptied(S[0], S[1])
            mark["attended", 2] = at_bank(S[1])

        def feed_forward():
            mark["up"] = [b.fills for b in A + V]
            first = PLACE["up", 2, 0]

            def chunk(q, loaded):
                s = (first + q) % NSLOT
                pe.wait_ge(ring_loaded[s], loaded)
                for f in range(2):
                    for part_, b in ((0, A[f]), (1, V[f])):
                        pe.wait_ge(b.free, b.fills)
                        for k in range(KD):
                            c0 = k * COLS + part_ * 256 + f * P
                            mm = pe.matmul(b.t[:, 0:SEQ], ring[s][:, c0:c0 + P], x2T[:, k, :], start=(k == 0), stop=(k == KD - 1))
                        mm.then_inc(b.full, b.fill())

            n_turn = UP_CHUNKS // NSLOT
            turns = Turns(*[(b, "fills", NSLOT) for b in (A[0], A[1], V[0], V[1])])
            with pe.Fori(0, n_turn) as i:
                turns.turn(i)
                for q in range(NSLOT):
                    chunk(q, 16 * ((first + q) // NSLOT + 1) + 16 * i)
            turns.done(n_turn)
            for q in range(n_turn * NSLOT, UP_CHUNKS):
                chunk(q, 16 * ((first + q) // NSLOT + 1))
            for b in V:
                pe.wait_ge(b.free, b.fills)
            for c in range(DOWN_CHUNKS):
                w = slot_of(("down", 2, c))
                for k in range(c * DOWN_K, min(FF_TILES, (c + 1) * DOWN_K)):
                    for tile in range(2):
                        for half in range(2):
                            c0 = k % DOWN_K * D + half * 512
                            mm = pe.matmul(V[2 * tile + half].t[:, :], hidden[:, k, tile * P:(tile + 1) * P], w[:, c0:c0 + 512],
                                           start=(k == 0), stop=(k == FF_TILES - 1))
                            if k == FF_TILES - 1:
                                mm.then_inc(V[2 * tile + half].full, V[2 * tile + half].fill())
                if c < DOWN_CHUNKS - 1:
                    mm.then_inc(down_used.sem, down_used.up())
                    mark["used", "down", 2, c] = (down_used.sem, down_used.n)

        pe.wait_ge(first_loaded, 32)
        for l in range(DEPTH):
            modulation(l)
            norm_columns(l)
            projections(l)
            differential(l)
            neighbourhood(l)
            merge(l)
            route(l)
            experts(l)
        norm2_columns(1)
        linear_attention_in()
        short_conv()
        linear_attention()
        dilated_in()
        linear_attention_out()
        dilated()
        pe.wait_ge(y_gla_done.sem, 1)
        emptied(V[2], V[3])
        merge(2, x2T, ys2T)
        mark["mix_out"] = (let_go(V[2]), let_go(V[3]))
        norm2_columns(2)
        feed_forward()
        mark["ff_out"] = [let_go(b) for b in V]

    @block.scalar
    def _(act):
        def evacuate(b, dst, func=ACT.Copy, n=512, shape=None, **kw):
            act.wait_ge(b.full, b.reads + 1)
            src = b.t[:, 0:n]
            if shape:
                src = src.rearrange("p (a n) -> p a n", a=shape)
            nc.scalar.activation(dst, src, func, **kw).then_inc(b.free, b.read())

        def modulation(l):
            nc.scalar.activation(cond[:, :, 0:2], col("cond").rearrange("p (k s) -> p k s", k=KD),
                                 ACT.Silu).then_inc(silu_done.sem, silu_done.up())
            def rows_squares():
                for tile in range(NT):
                    nc.scalar.activation(xhat[:, tile, :], h[:, tile, :], ACT.Square,
                                         accum_out=sq[:, tile:tile + 1]).then_inc(sq_done.sem, sq_done.up())

            for j in range(ADA_FIRST):
                evacuate(A[j % 2], ada_parts[:, j * COLS:(j + 1) * COLS])
            if l == 0:
                act.wait_ge(setup, 16 * SETUP)
                act.wait_ge(lam_prod.sem, 2)
                nc.scalar.activation(lam_s[:, :, :], lam_s[:, :, :], ACT.Exp).then_inc(lam_exp.sem, lam_exp.up())
                rows_squares()
            if l >= 1:
                act.wait_ge(h_done.sem, h_end(l - 1))
                rows_squares()

        def norm_columns(l):
            act.wait_ge(*mark["mod", l])
            for f in range(0, KD, 2):
                for s in range(2):
                    evacuate(A[s], xT[:, f, s * SEQ:(s + 1) * SEQ], ACT.Identity, n=SEQ,
                             scale=mod_a[:, f, s:s + 1], bias=mod_b[:, f, s:s + 1])

        def turned(br, nt, scale=None):
            for tile in range(nt):
                dst = ysT[:, br, :, tile * P:(tile + 1) * P]
                if scale is None:
                    evacuate(A[tile % 2], dst, shape=4)
                else:
                    evacuate(A[tile % 2], dst, ACT.Identity, shape=4, scale=scale)

        def columns_chunk(name, dst, n, scale):
            late = ADA_WITH[name]

            def whole_rows(j):
                kind, half = divmod(j - ADA_FIRST, 2)
                act.wait_ge(S[1].full, S[1].reads + 1)
                nc.scalar.activation(ada_rows[kind][:, half * COLS:(half + 1) * COLS], S[1].t[0:2, :], ACT.Copy)\
                    .then_inc(S[1].free, S[1].read())

            for f in range(4):
                if 0 < f <= len(late):
                    if f >= 2:
                        whole_rows(late[f - 2])
                    evacuate(S[0], tmp[:, :])
                evacuate(A[f % 2], dst[:, f, 0:n], n=n, scale=scale)
            whole_rows(late[-1])

        def projections(l):
            nt = tiles(l)
            for tile in range(nt):
                if tile >= 2:
                    act.wait_ge(*mark["yb", l, tile - 2])
                evacuate(A[0], u_sb[:, tile % 2, :], ACT.Gelu_apprx_tanh)
                evacuate(A[1], vv[:, tile % 2, :], ACT.Gelu_apprx_tanh)
            columns_chunk("KA", kaT, NT * P, 1.0)
            columns_chunk("QA", qaT, nt * P, 0.125)
            turned(1, nt)
            for tile in range(NT):
                evacuate(A[tile % 2], va[:, tile, :])
            act.wait_ge(rope_done.sem, 8 * (l + 1))
            columns_chunk("KC", kcT, NT * P, 1.0)
            act.wait_ge(modrow_done.sem, l + 1)
            for tile in range(NT):
                evacuate(A[tile % 2], vc[:, tile, :])
            for f in range(4):
                evacuate(A[f % 2], qcT[:, f, 0:nt * P], n=nt * P, scale=0.125)

        def n_keys(tile):
            return NT * P if tile < 2 else CTX

        def differential(l):
            items = [(tile, hd) for tile in range(tiles(l)) for hd in range(4)]
            base = sum(4 * tiles(k) for k in range(l))

            def exps(i):
                tile, hd = items[i]
                n = n_keys(tile)
                if i >= 2:
                    act.wait_ge(mix_done.sem, base + i - 1)
                for m in range(2):
                    q = 2 * (i % 2) + m
                    act.wait_ge(neg_max_done.sem, neg_max_done.take("act"))
                    nc.scalar.activation(probs[:, i % 2, m, 0:n], S[m].t[:, 0:n], ACT.Exp, bias=neg_max[:, q:q + 1],
                                         accum_out=exp_sum[:, q:q + 1]).then_inc(S[m].free, S[m].read())

            exps(0)
            for i in range(len(items)):
                if i + 1 < len(items):
                    exps(i + 1)
                kt = n_keys(items[i][0]) // P
                evacuate(A[i % 2], mixT[:, i % 2, 0:kt, :], n=kt * P, shape=kt)
            act.wait_ge(modrow_stored, 32 * (l + 1))
            turned(0, tiles(l), scale=sub_g[:, l:l + 1])

        def neighbourhood(l):
            items = [(tile, hd) for tile in range(tiles(l)) for hd in range(8)]

            def exps(i):
                tile, hd = items[i]
                n = n_keys(tile)
                if i >= 2:
                    act.wait_ge(*mark["turned", l, i - 2])
                if hd == 0 and tile >= 2:
                    act.wait_ge(*mark["o", l, tile - 2])
                act.wait_ge(neg_max_done.sem, neg_max_done.take("act"))
                src = mix[:, i % 2, :] if tile < 2 else S[i % 2].t[:, 0:n]
                ins = nc.scalar.activation(probs[:, i % 2, 0, 0:n], src, ACT.Exp, bias=neg_max[:, i % 2:i % 2 + 1],
                                           accum_out=na_sum[:, tile % 2, hd:hd + 1])
                if tile < 2:
                    ins.then_inc(p_done.sem, p_done.up())
                else:
                    ins.then_inc(S[i % 2].free, S[i % 2].read())

            exps(0)
            for i in range(len(items)):
                if i + 1 < len(items):
                    exps(i + 1)
                kt = n_keys(items[i][0]) // P
                evacuate(A[i % 2], mixT[:, i % 2, 0:kt, :], n=kt * P, shape=kt)
            turned(2, tiles(l))

        def merge(l):
            n = tiles(l) * P
            v0 = mark["merge", l][2:]
            turns = Turns((A[0], "reads", 6), (A[1], "reads", 6))
            with act.Fori(0, MERGE_CHUNKS // NSLOT) as i:
                turns.turn(i)
                for j in range(N_BR * NSLOT):
                    act.wait_ge(V[j % 2].free, v0[j % 2] + 6 * i + j // 2)
                    kw = {}
                    if l == DEPTH:
                        kw["bias"] = col("b_gate")[:, bass.ds(j % N_BR * MERGE_CHUNKS + NSLOT * i + j // N_BR, 1)]
                    evacuate(A[j % 2], gate_s[:, j % 2, 0:n], ACT.Sigmoid, n=n, **kw)
            turns.done(MERGE_CHUNKS // NSLOT)

        def second_norm(l):
            nt = tiles(l)
            for tile in range(nt):
                act.wait_ge(h_done.sem, h_done_mix(l) - nt + tile + 1)
                nc.scalar.activation(tmp_sq, h[:, tile, :], ACT.Square,
                                     accum_out=sq[:, tile:tile + 1]).then_inc(sq_done.sem, sq_done.up())
                act.wait_ge(sq_done.sem, sq_done.n)
            for tile in range(nt):
                for q in range(2):
                    evacuate(A[q], xT[:, 4 * q:4 * q + 4, tile * P:(tile + 1) * P], shape=4)
                act.wait_ge(xn2_done.sem, xn2_done.take("act"))
                act.dma_start(x_rows[l][tile * P:(tile + 1) * P, :], xn2[:, tile, :]).then_inc(x_stored[l], 16)
            for ap in (r_gexp[l], r_e2[l]):
                act.wait_ge(route_exp_in.sem, route_exp_in.take("act"))
                nc.scalar.activation(ap, ap, ACT.Exp).then_inc(route_exp_out.sem, route_exp_out.up())

        def expert(b, last=False):
            act.wait_ge(S[b].full, S[b].reads + 1)
            act.wait_ge(V[b].free, V[b].seen)
            nc.scalar.activation(silu_s[:, b, :], S[b].t[:, 0:D_HALF], ACT.Silu).then_inc(S[b].free, S[b].read())
            V[b].see()
            if not last:
                evacuate(A[1], xgT[:, 1 - b, :, :], shape=4)
            evacuate(A[0], hidT[:, b, :, :], n=D_HALF, shape=2)

        def experts(l):
            base = mark["moe", l]
            evacuate(A[1], xgT[:, 0, :, :], shape=4)
            for b in range(2):
                V[b].seen = base["V"][b]

            def turn(last):
                for q in range(MOE_AHEAD):
                    expert(q % 2, last and q == MOE_AHEAD - 1)

            n_turn = N_EXP // MOE_AHEAD
            turns = Turns((A[0], "reads", 4), (A[1], "reads", 4), (S[0], "reads", 2), (S[1], "reads", 2),
                          (V[0], "seen", 2), (V[1], "seen", 2))
            with act.Fori(0, n_turn - 1) as i:
                turns.turn(i)
                turn(False)
            turns.done(n_turn - 1)
            turn(True)
            with further_blocks(act, l) as j:
                s = xb[l]
                act.wait_ge(s["pe"], 4 * j + 1)
                nc.scalar.activation(xgT[:, 0, :, :], A[1].t[:, :].rearrange("p (a n) -> p a n", a=4), ACT.Copy)\
                    .then_inc(s["act"], 1)
                act.wait_ge(s["pe"], 4 * j + 2)
                nc.scalar.activation(silu_s[:, 0, :], S[0].t[:, 0:D_HALF], ACT.Silu).then_inc(s["act"], 1)
                act.wait_ge(s["pe"], 4 * j + 3)
                nc.scalar.activation(hidT[:, 0, :, :], A[0].t[:, 0:D_HALF].rearrange("p (a n) -> p a n", a=2), ACT.Copy)\
                    .then_inc(s["act"], 1)

        def squares(src, junk, done=None):
            for tile in range(2):
                if done:
                    act.wait_ge(done[0], done[1] + tile + 1)
                if tile:
                    act.wait_ge(sq_done.sem, sq_done.n)
                nc.scalar.activation(junk, src[:, tile, :], ACT.Square,
                                     accum_out=sq[:, tile:tile + 1]).then_inc(sq_done.sem, sq_done.up())

        def norm2_columns(gain):
            for f in range(KD):
                evacuate(A[f % 2], x2T[:, f, :], ACT.Identity, n=SEQ, scale=col(gain)[:, f:f + 1])

        def linear_attention_in():
            for f in range(4):
                evacuate(A[f % 2], gqkT[:, f, :], n=SEQ, scale=64 ** -0.5 if f < 2 else 1.0)
            act.wait_ge(A[0].full, A[0].reads + 1)
            nc.scalar.activation(alowT, A[0].t[0:GLA_RANK, 0:SEQ], ACT.Copy).then_inc(A[0].free, A[0].read())
            for tile in range(2):
                evacuate(A[tile], gv[:, tile, :])
            act.wait_ge(rope_in.sem, 1)
            nc.scalar.activation(sin2, sin_in, ACT.Sin)
            nc.scalar.activation(cos2, cos_in, ACT.Sin, bias=C("half_pi")).then_inc(rope_table.sem, rope_table.up())
            act.wait_ge(alow_exp_in.sem, 1)
            nc.scalar.activation(kinT, kinT, ACT.Exp).then_inc(alow_exp_out.sem, alow_exp_out.up())
            act.wait_ge(alow_exp_out.sem, 1)
            nc.scalar.activation(kinT, kinT, ACT.Ln, bias=1.0).then_inc(alow_exp_out.sem, alow_exp_out.up())
            for f in range(4):
                evacuate(A[f % 2], g2T[:, f, :], ACT.Silu, n=SEQ)
            s = 1 / GLA_TAU
            act.wait_ge(decay_in.sem, 1)
            ends = kinT.rearrange("p f (c n) -> p f c n", n=GLA_CHUNK)[:, :, :, GLA_CHUNK - 1]
            nc.scalar.activation(decay, ends, ACT.Exp, scale=s)
            nc.scalar.activation(qinT, kinT, ACT.Exp, scale=s).then_inc(decay_out.sem, decay_out.up())
            act.wait_ge(decay_in.sem, 2)
            nc.scalar.activation(kin_rows.rearrange("p t n -> p (t n)"), log_a.rearrange("p f n -> p (f n)"), ACT.Exp,
                                 scale=-s).then_inc(decay_out.sem, decay_out.up())
            nc.scalar.activation(log_a, log_a, ACT.Exp, scale=s).then_inc(decay_out.sem, decay_out.up())
            act.wait_ge(decay_in.sem, 3)
            nc.scalar.activation(end_gap, end_gap, ACT.Exp, scale=-s).then_inc(decay_out.sem, decay_out.up())
            for f in range(4):
                evacuate(A[f % 2], conv_in[:, f, 2:], n=SEQ)

        def linear_attention():
            evacuate(A[0], kin_rows, shape=2)

        def dilated_in():
            for i in range(3):
                for tile in range(2):
                    evacuate(A[tile], dv[:, tile, i * COLS:(i + 1) * COLS])
            for dst in (dqT, dkT):
                for i in range(3):
                    for f in range(4):
                        evacuate(A[f % 2], dst[:, 4 * i + f, :], n=SEQ)

        def dilated():
            items = [(tile, hd) for tile in range(2) for hd in range(4)]

            def exps(i):
                n = 3 * (items[i][0] + 1) * P
                if i >= 2:
                    act.wait_ge(*mark["d_turned", i - 2])
                act.wait_ge(d_max_done.sem, i + 1)
                nc.scalar.activation(d_p[:, i % 2, 0:n], d_sc[:, i % 2, 0:n], ACT.Exp, bias=d_max[:, i % 2:i % 2 + 1],
                                     accum_out=d_sum[:, i % 2:i % 2 + 1]).then_inc(d_exp_done.sem, d_exp_done.up())

            def out(i):
                tile, hd = items[i]
                evacuate(S[i % 2], ys2T[:, 2, hd, tile * P:(tile + 1) * P], n=P)

            exps(0)
            for i in range(len(items)):
                if i + 1 < len(items):
                    exps(i + 1)
                n = 3 * (items[i][0] + 1)
                for b in range(-(-n // 4)):
                    m = min(4, n - 4 * b)
                    evacuate(A[b], d_pT[:, i % 2, 4 * b:4 * b + m, :], n=m * P, shape=m)
                if i >= 1:
                    out(i - 1)
            out(len(items) - 1)

        def feed_forward():
            turns = Turns((A[0], "reads", 1), (A[1], "reads", 1), (gelu_done, "n", 2))
            with act.Fori(0, UP_CHUNKS) as i:
                turns.turn(i)
                for f in range(2):
                    evacuate(A[f], gate_in[:, f, 2:], n=SEQ)
                for f in range(2):
                    act.wait_ge(conv_done.sem, 2 * i + f + 1)
                    nc.scalar.activation(conved[:, f, :], conved[:, f, :], ACT.Gelu_apprx_tanh,
                                         bias=col("ff_conv_b")[:, bass.ds(2 * i + f, 1)]).then_inc(gelu_done.sem, gelu_done.up())
            turns.done(UP_CHUNKS)

        act.wait_ge(first_loaded, 32)
        for l in range(DEPTH):
            modulation(l)
            norm_columns(l)
            projections(l)
            differential(l)
            neighbourhood(l)
            merge(l)
            second_norm(l)
            experts(l)
        squares(h, tmp_sq, (h_done.sem, h_end(DEPTH - 1) - 2))
        squares(h, tmp_sq, (final_done.sem, 0))
        norm2_columns("pre_mix_g")
        linear_attention_in()
        linear_attention()
        dilated_in()
        dilated()
        merge(DEPTH)
        for w in mark["mix_out"]:
            act.wait_ge(*w)
        squares(y2, work[:, 0:1024])
        squares(h, tmp_sq, (x_done.sem, 0))
        norm2_columns("pre_ffn_g")
        feed_forward()
        for w in mark["ff_out"]:
            act.wait_ge(*w)
        squares(y2, work[:, 0:1024])

    @block.vector
    def _(dve):
        def step(ins):
            ins.then_inc(dve_step.sem, dve_step.up())
            dve.wait_ge(dve_step.sem, dve_step.n)

        def power(ins):
            ins.then_inc(pow_in.sem, pow_in.up())
            dve.wait_ge(pow_out.sem, pow_in.n)

        TT, TS, STT = nc.vector.tensor_tensor, nc.vector.tensor_scalar, nc.vector.scalar_tensor_tensor

        def zero_conditions():
            nc.vector.memset(cond[:, :, 2:], 0.0).then_inc(cond_zero.sem, cond_zero.up())

        def setup_scalars():
            prod = tmp[:, 0:DEPTH * 2 * 64].rearrange("p (l m n) -> p l m n", l=DEPTH, m=2)
            for l in range(DEPTH):
                pair = lam_in[:, l, :, :].rearrange("p (m r) n -> p m r n", r=2)
                step(TT(prod[:, l, :, :], pair[:, :, 0, :], pair[:, :, 1, :], ALU.mult))
                nc.vector.tensor_reduce(lam_s[:, l, :], prod[:, l, :, :], X, ALU.add).then_inc(lam_prod.sem, lam_prod.up())
            dve.wait_ge(lam_exp.sem, 1)
            for l in range(DEPTH):
                init = 0.8 - 0.6 * math.exp(-0.3 * l)
                step(STT(out=neglam[:, l:l + 1], in0=lam_s[:, l, 1:2], scalar=init, in1=lam_s[:, l, 0:1],
                         op0=ALU.subtract, op1=ALU.subtract))
                step(TS(sub_g[:, l:l + 1], col("sub_g", l), 1.0 - init, None, ALU.mult))

        def modulation(l):
            dve.wait_ge(sq_done.sem, sq_done.take("dve", NT))
            power(TS(rstd[:, :], sq[:, :], 1.0 / D, EPS, ALU.mult, ALU.add))
            for tile in range(NT):
                TS(xhat[:, tile, :], h[:, tile, :], rstd[:, tile:tile + 1], None, ALU.mult)\
                    .then_inc(xhat_done.sem, xhat_done.up())
            b = V[0]
            dve.wait_ge(b.full, b.reads + 1)
            both = b.t[:, 0:4 * KD].rearrange("p (c k s) -> p c k s", c=2, k=KD)
            nc.vector.tensor_copy(mod_b[:, :, :], both[:, 0])
            STT(out=mod_a[:, :, :], in0=both[:, 1], scalar=1.0,
                in1=col("g1", l).unsqueeze(2).to_broadcast([P, KD, 2]), op0=ALU.add, op1=ALU.mult)\
                .then_inc(b.free, b.read())
            dve.wait_ge(b.free, b.reads)

        def second_scale(l):
            for b in S:
                b.seen = b.seen + ADA_CHUNKS - ADA_FIRST
            dve.wait_ge(*mark["ada", l])
            dve.wait_ge(rows_in[l], 64)
            sc2 = ada_rows[2]
            STT(out=sc2, in0=sc2, scalar=1.0, in1=g2row, op0=ALU.add, op1=ALU.mult)\
                .then_inc(modrow_done.sem, modrow_done.up())

        def norm_columns(l):
            for f in range(1, KD, 2):
                for s in range(2):
                    b = V[s]
                    dve.wait_ge(b.full, b.reads + 1)
                    TS(xT[:, f, s * SEQ:(s + 1) * SEQ], b.t[:, 0:SEQ], mod_a[:, f, s:s + 1], mod_b[:, f, s:s + 1],
                       ALU.mult, ALU.add).then_inc(b.free, b.read())

        def projections(l):
            nt = tiles(l)

            def normed(tile):
                v = vv[:, tile % 2, :]
                dve.wait_ge(*mark["v", l, tile])
                step(nc.vector.bn_stats(bn6, v))
                step(nc.vector.bn_aggr(bn2, bn6))
                power(TS(ln_var, bn2[:, 1:2], EPS, None, ALU.add))
                step(TS(v, v, bn2[:, 0:1], ln_r, ALU.subtract, ALU.mult))
                step(TT(v, v, ln_rows[:, 0, :], ALU.mult))
                TT(v, v, ln_rows[:, 1, :], ALU.add).then_inc(vv_done.sem, vv_done.up())

            def gated(tile):
                b = V[tile % 2]
                dve.wait_ge(b.full, b.reads + 1)
                dve.wait_ge(*mark["u", l, tile])
                for g in range(4):
                    c = slice(g * P, (g + 1) * P)
                    ins = STT(out=yb[:, tile, c], in0=b.t[:, c], scalar=col("sg_b", l)[:, g:g + 1],
                              in1=u_sb[:, tile % 2, c], op0=ALU.add, op1=ALU.mult)
                ins.then_inc(b.free, b.read())

            dve.wait_ge(rows_in[l], 64)
            for tile in range(nt):
                normed(tile)
                if tile >= 1:
                    gated(tile - 1)
            gated(nt - 1)
            for w in mark["qk", l]:
                dve.wait_ge(*w)
            for i in range(8):
                b = V[i % 2]
                x = (kaT if i < 4 else qaT)[:, i % 4, 0:SEQ]
                dve.wait_ge(b.full, b.reads + 1)
                TT(tmp[:, 0:SEQ], b.t[:, 0:SEQ], C("sin_axial"), ALU.mult).then_inc(b.free, b.read())
                step(TT(x, x, C("cos_axial"), ALU.mult))
                dve.wait_ge(b.free, b.reads)
                TT(x, x, tmp[:, 0:SEQ], ALU.add).then_inc(rope_done.sem, rope_done.up())
                dve.wait_ge(rope_done.sem, rope_done.n)
            second_scale(l)

        def n_keys(tile):
            return NT * P if tile < 2 else CTX

        def negmax(dst, src):
            nc.vector.tensor_reduce(dst, src, X, ALU.max, negate=True).then_inc(neg_max_done.sem, neg_max_done.up())

        def differential(l):
            items = [(tile, hd) for tile in range(tiles(l)) for hd in range(4)]

            def maxima(i):
                for m in range(2):
                    dve.wait_ge(S[m].full, S[m].see())
                    negmax(neg_max[:, 2 * (i % 2) + m:2 * (i % 2) + m + 1], S[m].t[:, 0:n_keys(items[i][0])])

            def mixed(i):
                n = n_keys(items[i][0])
                q = 2 * (i % 2)
                for m in range(2):
                    dve.wait_ge(S[m].free, S[m].seen)
                step(nc.vector.reciprocal(inv_sum[:, q:q + 2], exp_sum[:, q:q + 2]))
                step(TS(inv_sum[:, q + 1:q + 2], inv_sum[:, q + 1:q + 2], neglam[:, l:l + 1], None, ALU.mult))
                p1 = probs[:, i % 2, 1, 0:n]
                step(TS(p1, p1, inv_sum[:, q + 1:q + 2], None, ALU.mult))
                if i >= 2:
                    dve.wait_ge(*mark["mixed", l, i - 2])
                STT(out=mix[:, i % 2, 0:n], in0=probs[:, i % 2, 0, 0:n], scalar=inv_sum[:, q:q + 1], in1=p1,
                    op0=ALU.mult, op1=ALU.add).then_inc(mix_done.sem, mix_done.up())

            def normed(tile):
                b = V[tile % 2]
                o = o_rows[:, tile, :]
                dve.wait_ge(b.full, b.reads + 1)
                nc.vector.tensor_copy(o, b.t[:, :]).then_inc(b.free, b.read())
                dve.wait_ge(b.free, b.reads)
                step(TT(tmp[:, 0:512], o, o, ALU.mult))
                step(nc.vector.tensor_reduce(head_sq, tmp[:, 0:512].rearrange("p (h n) -> p h n", h=4), X, ALU.add))
                power(TS(head_sq, head_sq, 1.0 / P, EPS, ALU.mult, ALU.add))
                o4 = o.rearrange("p (h n) -> p h n", h=4)
                TT(o4, o4, head_r.unsqueeze(2).to_broadcast([P, 4, P]), ALU.mult).then_inc(o_done.sem, o_done.up())

            maxima(0)
            for i, (tile, hd) in enumerate(items):
                mixed(i)
                if i + 1 < len(items):
                    maxima(i + 1)
                if hd == 0 and tile >= 1:
                    normed(tile - 1)
            normed(tiles(l) - 1)

        def neighbourhood(l):
            items = [(tile, hd) for tile in range(tiles(l)) for hd in range(8)]
            c = PLACE["bias", l, 0]
            bias = ring[c % NSLOT][:, 0:4096].rearrange("p (h t n) -> p h t n", h=8, t=2)
            p0 = 16 * l

            def scored(i):
                tile, hd = items[i]
                nm = neg_max[:, i % 2:i % 2 + 1]
                if tile >= 2:
                    dve.wait_ge(S[i % 2].full, S[i % 2].see())
                    if i < 18:
                        dve.wait_ge(p_done.sem, p0 + i - 1)
                    negmax(nm, S[i % 2].t[:, 0:CTX])
                    return
                b = V[i % 2]
                dve.wait_ge(b.full, b.reads + 1)
                if i >= 2:
                    dve.wait_ge(p_done.sem, p0 + i - 1)
                TT(mix[:, i % 2, 0:SEQ], b.t[:, 0:SEQ], bias[:, hd, tile, :], ALU.add)
                nc.vector.tensor_copy(mix[:, i % 2, SEQ:], b.t[:, SEQ:]).then_inc(b.free, b.read())
                dve.wait_ge(b.free, b.reads)
                negmax(nm, mix[:, i % 2, :])

            def normed(tile):
                b = V[2 + tile % 2]
                dve.wait_ge(b.full, b.reads + 1)
                step(nc.vector.reciprocal(na_inv[:, tile % 2, :], na_sum[:, tile % 2, :]))
                TT(o_rows[:, tile, :].rearrange("p (h n) -> p h n", h=8), b.t[:, :].rearrange("p (h n) -> p h n", h=8),
                   na_inv[:, tile % 2, :].unsqueeze(2).to_broadcast([P, 8, 64]), ALU.mult).then_inc(b.free, b.read())

            dve.wait_ge(ring_loaded[c % NSLOT], 16 * (c // NSLOT + 1))
            for w in mark["da_turned", l]:
                dve.wait_ge(*w)
            for i, (tile, hd) in enumerate(items):
                scored(i)
                if hd == 2 and tile >= 1:
                    normed(tile - 1)
            normed(tiles(l) - 1)

        def merge(l):
            n = tiles(l) * P
            a0, a1 = mark["merge", l][:2]
            turns = Turns((V[0], "reads", 6), (V[1], "reads", 6), (merge_done, "n", 2 * NSLOT))
            with dve.Fori(0, MERGE_CHUNKS // NSLOT) as i:
                turns.turn(i)
                for dd in range(NSLOT):
                    acc = merged[:, bass.ds(NSLOT * i + dd, 1), 0:n].rearrange("p k n -> p (k n)")
                    for br in range(N_BR):
                        j = N_BR * dd + br
                        b = V[j % 2]
                        dve.wait_ge(b.full, b.reads + 1)
                        dve.wait_ge(A[j % 2].free, (a0, a1)[j % 2] + 6 * i + j // 2 + 1)
                        dst = acc if br == 0 else part[:, br - 1, 0:n]
                        TT(dst, gate_s[:, j % 2, 0:n], b.t[:, 0:n], ALU.mult).then_inc(b.free, b.read())
                        if br >= 1:
                            dve.wait_ge(b.free, b.reads)
                            if br == 2:
                                dve.wait_ge(merge_done.sem, merge_done.n)
                            TT(acc, acc, part[:, br - 1, 0:n], ALU.add).then_inc(merge_done.sem, merge_done.up())
            turns.done(MERGE_CHUNKS // NSLOT)

        def mix_out(l):
            dve.wait_ge(mods_in[l], 64)
            for c in range(OUT_CHUNKS):
                for tile in range(tiles(l)):
                    b = V[2 + tile % 2]
                    half = slice(c * COLS, (c + 1) * COLS)
                    q = part[:, tile % 2, :]
                    dve.wait_ge(b.full, b.reads + 1)
                    TT(q, b.t[:, :], gt1b[:, tile // 2, half], ALU.mult).then_inc(b.free, b.read())
                    dve.wait_ge(b.free, b.reads)
                    TT(h[:, tile, half], h[:, tile, half], q, ALU.add).then_inc(h_done.sem, h_done.up())

        def second_norm(l):
            nt = tiles(l)
            dve.wait_ge(sq_done.sem, sq_done.take("dve", nt))
            power(TS(rstd[:, 0:nt], sq[:, 0:nt], 1.0 / D, EPS, ALU.mult, ALU.add))
            for tile in range(nt):
                s = tile // 2
                step(STT(out=xn2[:, tile, :], in0=h[:, tile, :], scalar=rstd[:, tile:tile + 1], in1=a2b[:, s, :],
                         op0=ALU.mult, op1=ALU.mult))
                TT(xn2[:, tile, :], xn2[:, tile, :], sh2b[:, s, :], ALU.add).then_inc(xn2_done.sem, xn2_done.up())

        def route(l):
            nt = tiles(l)
            at = [nt * N_EXP]

            def area(n, shape=True):
                a = at[0]
                at[0] += nt * n
                return rt[:, a:a + nt * n].rearrange("p (t n) -> p t n", t=nt)

            def one(n):
                return area(n)

            pick = rt[:, 0:nt * N_EXP].rearrange("p (t e) -> p t e", t=nt)
            logits = r_logits[l]
            iota = C("iota").unsqueeze(1).to_broadcast([P, nt, N_EXP])
            iota4 = C("iota")[:, 0:N_GRP].unsqueeze(1).to_broadcast([P, nt, N_GRP])
            b = V[0]
            dve.wait_ge(b.full, b.reads + 1)
            nc.vector.tensor_copy(logits, b.t[:, 0:nt * 36].rearrange("p (t n) -> p t n", t=nt)).then_inc(b.free, b.read())
            dve.wait_ge(b.free, b.reads)

            def first_max(v, io, n, r):
                mx, ne, cand, idx, hot = r
                wide = [P, nt, n]
                step(nc.vector.tensor_reduce(mx, v, X, ALU.max))
                step(TT(ne, v, mx.to_broadcast(wide), ALU.not_equal))
                step(STT(out=cand, in0=ne, scalar=64.0, in1=io, op0=ALU.mult, op1=ALU.add))
                step(nc.vector.tensor_reduce(idx, cand, X, ALU.min))
                step(TT(hot, io, idx.to_broadcast(wide), ALU.is_equal))

            r = r_area[l]
            grp, exps = logits[:, :, 0:N_GRP], logits[:, :, N_GRP:]
            first_max(grp, iota4, N_GRP, (r["gmax"], r["g1"], r["g2"], r["gidx"], r["ghot"]))
            TT(r_gexp[l], grp, r["gmax"].to_broadcast([P, nt, N_GRP]), ALU.subtract)\
                .then_inc(route_exp_in.sem, route_exp_in.up())
            hot8 = r["ghot"].unsqueeze(3).to_broadcast([P, nt, N_GRP, PER_GRP])
            e4 = exps.rearrange("p t (g e) -> p t g e", g=N_GRP)
            s4 = r["sel"].rearrange("p t (g e) -> p t g e", g=N_GRP)
            step(TT(s4, e4, hot8, ALU.mult))
            step(TS(r["ghot"], r["ghot"], 1.0, -NEG, ALU.subtract, ALU.mult))
            step(TT(s4, s4, hot8, ALU.add))
            first_max(r["sel"], iota, N_EXP, (r["m1"], r["w1"], r["w2"], r["i1"], r["hot1"]))
            step(STT(out=r["sel"], in0=r["hot1"], scalar=2 * NEG, in1=r["sel"], op0=ALU.mult, op1=ALU.add))
            first_max(r["sel"], iota, N_EXP, (r["m2"], r["w1"], r["w2"], r["i2"], r["hot2"]))
            TT(r_e2[l], r["m2"], r["m1"], ALU.subtract).then_inc(route_exp_in.sem, route_exp_in.up())
            TT(pick, r["hot1"], r["hot2"], ALU.add).then_inc(picked.sem, picked.up())
            dve.wait_ge(route_exp_out.sem, 2 * (l + 1))
            step(nc.vector.tensor_reduce(r["gsum"], r_gexp[l], X, ALU.add))
            step(TS(r["den"], r_e2[l], 1.0, None, ALU.add))
            step(TT(r["den"], r["den"], r["gsum"], ALU.mult))
            step(nc.vector.reciprocal(weight[:, 0:nt, 0:1], r["den"]))
            step(TT(weight[:, 0:nt, 1:2], weight[:, 0:nt, 0:1], r_e2[l], ALU.mult))
            b = V[1]
            dve.wait_ge(b.full, b.reads + 1)
            rank = b.t[:, 0:nt * N_EXP].rearrange("p (t e) -> p t e", t=nt)
            for k, hot in ((0, r["hot1"]), (1, r["hot2"])):
                step(TT(r["w1"], hot, rank, ALU.mult))
                step(nc.vector.tensor_reduce(r["pos"][:, :, k:k + 1], r["w1"], X, ALU.add))
            nc.vector.tensor_copy(r["cnt"], b.t[:, NT * N_EXP:(NT + 1) * N_EXP]).then_inc(b.free, b.read())
            pos, blk = r["pos"], r["blk"]
            step(TS(blk, pos, float(CAP), None, ALU.is_ge))
            for n in range(2, N_BLK):
                step(STT(out=blk, in0=pos, scalar=float(n * CAP), in1=blk, op0=ALU.is_ge, op1=ALU.add))
            step(STT(out=pos, in0=blk, scalar=float(-CAP), in1=pos, op0=ALU.mult, op1=ALU.add))
            for k, idx in ((0, r["i1"]), (1, r["i2"])):
                step(STT(out=blk[:, :, k:k + 1], in0=blk[:, :, k:k + 1], scalar=float(N_EXP), in1=idx, op0=ALU.mult, op1=ALU.add))
            halves = C("places")[:, 0:CAP].unsqueeze(1).to_broadcast([P, 2, CAP])
            for tile in range(nt):
                for k in range(2):
                    q = 2 * tile + k
                    TS(hot_slot[:, q, :].rearrange("p (h n) -> p h n", h=2), halves, pos[:, tile, k:k + 1], None, ALU.is_equal)
                    TS(hot_place[:, q, :], C("places"), blk[:, tile, k:k + 1], C("half_row")[:, q:q + 1], ALU.is_equal, ALU.mult)\
                        .then_inc(hot_done.sem, hot_done.up())
            b = V[2]
            dve.wait_ge(b.full, b.reads + 1)
            TS(table[:, :], b.t[:, 0:N_BLK * N_EXP], float(NOLIMIT), None, ALU.add).then_inc(b.free, b.read())
            dve.wait_ge(b.free, b.reads)
            step(TS(token_of[:, :], table[:, :], 2, None, ALU.arith_shift_right))
            step(TS(token_of[:, :], token_of[:, :], nt * P - 1, 2, ALU.min, ALU.mult))
            TS(token_of[CAP:, :], token_of[CAP:, :], 1, None, ALU.add)
            TS(table[CAP:, :], table[CAP:, :], 1, None, ALU.add).then_inc(token_done.sem, token_done.up())
            list_further(l)
            if l < DEPTH - 1:
                zero_conditions()

        def list_further(l):
            r, n = r_area[l], further(l)
            blocks, upto = r["x_blocks"], r["x_upto"]
            gap, hot, val = [r["x_" + k].rearrange("p (j e) -> p j e", j=n) for k in ("gap", "hot", "val")]
            wide = [1, n, N_EXP]
            iota = C("iota")[0:1, :]
            per_expert = iota.unsqueeze(1).to_broadcast(wide)
            cnt = r["cnt"][0:1, :]
            step(TS(blocks, cnt, float(CAP + 1), None, ALU.is_ge))
            for k in range(2, N_BLK):
                step(STT(out=blocks, in0=cnt, scalar=float(k * CAP + 1), in1=blocks, op0=ALU.is_ge, op1=ALU.add))
            step(nc.vector.tensor_tensor_scan(upto, ones[0:1, 0:N_EXP], blocks, 0.0, ALU.mult, ALU.add))
            number = upto[:, N_EXP - 1:N_EXP]
            step(nc.vector.tensor_copy(r["x_list"][:, 0:1], number))
            step(TT(upto, upto, blocks, ALU.subtract))
            step(TT(gap, iota[:, 0:n].unsqueeze(2).to_broadcast(wide), upto.unsqueeze(1).to_broadcast(wide), ALU.subtract))
            step(TT(hot, gap, blocks.unsqueeze(1).to_broadcast(wide), ALU.is_lt))
            step(STT(out=hot, in0=gap, scalar=0.0, in1=hot, op0=ALU.is_ge, op1=ALU.mult))
            step(STT(out=val, in0=gap, scalar=float(N_EXP), in1=per_expert, op0=ALU.mult, op1=ALU.add))
            step(TS(val, val, float(N_EXP), None, ALU.add))
            step(TT(val, val, hot, ALU.mult))
            step(TT(hot, hot, per_expert, ALU.mult))
            pair = r["x_pair"].rearrange("p (j k) -> p j k", k=2)
            step(nc.vector.tensor_reduce(pair[:, :, 0:1], hot, X, ALU.add))
            step(nc.vector.tensor_reduce(pair[:, :, 1:2], val, X, ALU.add))
            nc.vector.tensor_copy(r["x_list"][:, 1:], r["x_pair"]).then_inc(xb[l]["list"], 1)

        def expert(b):
            dve.wait_ge(V[b].full, V[b].reads + 1)
            dve.wait_ge(S[b].free, S[b].see())
            TT(hid[:, b, :], silu_s[:, b, :], V[b].t[:, 0:D_HALF], ALU.mult).then_inc(V[b].free, V[b].read())

        def experts(l):
            for b in range(2):
                S[b].seen = mark["moe", l]["S"][b]

            def turn(i):
                for q in range(MOE_AHEAD):
                    expert(q % 2)
                    n = N_EXP // 2 * l + q // 2 + 2 * i
                    if not isinstance(n, int) or n > N_EXP // 2 * l:
                        dve.wait_ge(scattered[q % 2], 16 * n)
                    o = V[2 + q % 2]
                    dve.wait_ge(o.full, o.reads + 1)
                    nc.vector.tensor_copy(y_sb[:, q % 2, :], o.t[:, :]).then_inc(o.free, o.read())

            turn(0)
            turns = Turns(*[(b, "reads", 2) for b in V], (S[0], "seen", 2), (S[1], "seen", 2))
            with dve.Fori(1, N_EXP // MOE_AHEAD) as i:
                turns.turn(i - 1)
                turn(i)
            turns.done(N_EXP // MOE_AHEAD - 1)
            with further_blocks(dve, l) as j:
                s, r = xb[l], r_area[l]
                c = dve.value_load(r["x_list"][:, bass.ds(2 * j + 2, 1)], min_val=0, max_val=N_BLK * N_EXP - 1)
                dve.wait_ge(scattered[0], 16 * (N_EXP // 2) * (l + 1))
                nc.vector.tensor_copy(r["x_ids"][:, 0:1], token_of[:, bass.ds(c, 1)])
                nc.vector.tensor_copy(r["x_ids"][:, 1:2], table[:, bass.ds(c, 1)]).then_inc(s["index"], 1)
                dve.wait_ge(s["act"], 3 * j + 2)
                TT(hid[:, 0, :], silu_s[:, 0, :], V[0].t[:, 0:D_HALF], ALU.mult).then_inc(s["dve"], 1)
                dve.wait_ge(s["pe"], 4 * j + 4)
                nc.vector.tensor_copy(y_sb[:, 0, :], V[2].t[:, :]).then_inc(s["dve"], 1)
                dve.wait_ge(s["sent"], 16 * j + 16)
                dve.sem_inc(s["passed"], 1)

        def combine(l):
            for tile in range(tiles(l)):
                y = ybuf[:, tile % 2, :].rearrange("p (k n) -> p k n", k=2)
                dve.wait_ge(y_in[tile % 2], 16 * (1 + sum(tiles(k) // 2 for k in range(l)) + tile // 2))
                step(TS(y[:, 0, :], y[:, 0, :], weight[:, tile, 0:1], None, ALU.mult))
                step(STT(out=y[:, 0, :], in0=y[:, 1, :], scalar=weight[:, tile, 1:2], in1=y[:, 0, :],
                         op0=ALU.mult, op1=ALU.add))
                step(TT(y[:, 0, :], y[:, 0, :], gt2b[:, tile // 2, :], ALU.mult))
                TT(h[:, tile, :], h[:, tile, :], y[:, 0, :], ALU.add).then_inc(h_done.sem, h_done.up())

        def root_mean():
            dve.wait_ge(sq_done.sem, sq_done.take("dve", 2))
            power(TS(rstd[:, 0:2], sq[:, 0:2], 1.0 / D, EPS, ALU.mult, ALU.add))

        def final_norm():
            root_mean()
            dve.wait_ge(block2_in[1], 32)
            for tile in range(2):
                STT(out=h[:, tile, :], in0=h[:, tile, :], scalar=rstd[:, tile:tile + 1], in1=final_g, op0=ALU.mult,
                    op1=ALU.mult).then_inc(final_done.sem, final_done.up())
            dve.wait_ge(final_done.sem, 2)

        def rows_norm():
            root_mean()
            for tile in range(2):
                TS(x2hat[:, tile, :], h[:, tile, :], rstd[:, tile:tile + 1], None, ALU.mult)\
                    .then_inc(xhat_done.sem, xhat_done.up())

        def rope_tables():
            part1, part2 = 6.28125, 0.0019350051879882812
            part3 = 2 * math.pi - part1 - part2
            magic = 1.5 * 2.0 ** 23
            dve.wait_ge(block2_in[0], 16 * 4)
            nc.vector.memset(conv_in[:, :, 0:2], 0.0)
            step(nc.vector.tensor_copy(ang, pos_i))
            step(TS(ang, ang, C("inv_freq"), None, ALU.mult))
            step(TS(turns_of, ang, 1 / (2 * math.pi), magic, ALU.mult, ALU.add))
            step(TS(turns_of, turns_of, magic, None, ALU.subtract))
            step(STT(out=sin_in, in0=turns_of, scalar=-part1, in1=ang, op0=ALU.mult, op1=ALU.add))
            step(STT(out=sin_in, in0=turns_of, scalar=-part2, in1=sin_in, op0=ALU.mult, op1=ALU.add))
            step(STT(out=sin_in, in0=turns_of, scalar=-part3, in1=sin_in, op0=ALU.mult, op1=ALU.add))
            step(TS(sin_in, sin_in, 3.1415925, -3.1415925, ALU.min, ALU.max))
            STT(out=cos_in, in0=sin_in, scalar=-1.0, in1=sin_in, op0=ALU.mult, op1=ALU.min)\
                .then_inc(rope_in.sem, rope_in.up())

        def forget_gates():
            b = V[0]
            dve.wait_ge(b.full, b.reads + 1)
            for f in range(2):
                ins = TS(log_a[:, f, :], b.t[:, f * SEQ:(f + 1) * SEQ], col("b_alpha")[:, f:f + 1], None, ALU.add)
            ins.then_inc(b.free, b.read())
            dve.wait_ge(b.free, b.reads)
            STT(out=kinT, in0=log_a, scalar=-1.0, in1=log_a, op0=ALU.mult, op1=ALU.min)\
                .then_inc(alow_exp_in.sem, alow_exp_in.up())
            dve.wait_ge(alow_exp_out.sem, 2)
            step(STT(out=log_a, in0=log_a, scalar=0.0, in1=kinT, op0=ALU.min, op1=ALU.subtract))
            for f in range(2):
                ins = nc.vector.tensor_tensor_scan(kinT[:, f, :], C("carry"), log_a[:, f, :], 0.0, ALU.mult, ALU.add)
            ins.then_inc(decay_in.sem, decay_in.up())
            dve.wait_ge(decay_in.sem, 1)
            wide = [P, 2 * SEQ // GLA_CHUNK, GLA_CHUNK]
            lc, la, gap = [v.rearrange("p f n -> p (f n)").rearrange("p (c n) -> p c n", n=GLA_CHUNK)
                           for v in (kinT, log_a, end_gap)]
            mid = GLA_CHUNK // 2 - 1
            step(TT(la, lc, lc[:, :, mid:mid + 1].to_broadcast(wide), ALU.subtract))
            TS(log_a, log_a, 80.0 * GLA_TAU, -80.0 * GLA_TAU, ALU.min, ALU.max).then_inc(decay_in.sem, decay_in.up())
            TT(gap, lc, lc[:, :, GLA_CHUNK - 1:].to_broadcast(wide), ALU.subtract).then_inc(decay_in.sem, decay_in.up())
            for w in mark["gqk"]:
                dve.wait_ge(*w)
            dve.wait_ge(decay_out.sem, 1)
            TT(qinT, qinT, gqkT[:, 0:2, :], ALU.mult).then_inc(gla_cols.sem, gla_cols.up())
            dve.wait_ge(decay_out.sem, 4)
            TT(kinT, end_gap, gqkT[:, 2:4, :], ALU.mult).then_inc(gla_cols.sem, gla_cols.up())
            TT(gqkT[:, 0:2, :], gqkT[:, 0:2, :], log_a, ALU.mult).then_inc(gla_cols.sem, gla_cols.up())
            keys = gqkT[:, 2:4, :].rearrange("p f n -> p (f n)")
            TT(keys, keys, kin_rows.rearrange("p t n -> p (t n)"), ALU.mult).then_inc(gla_cols.sem, gla_cols.up())

        def short_conv():
            for w in mark["sc"]:
                dve.wait_ge(*w)
            for f in range(4):
                b = V[2 + f % 2]
                dve.wait_ge(b.full, b.reads + 1)
                u = conv_in[:, f, 2:]
                TT(u, u, b.t[:, 0:SEQ], ALU.mult).then_inc(b.free, b.read())
                dve.wait_ge(b.free, b.reads)
            taps = col("sc_conv_w")
            y = ys2T[:, 1]
            for f in range(4):
                ins = TS(y[:, f, :], conv_in[:, f, 0:SEQ], taps[:, f:f + 1], None, ALU.mult)
            step(ins)
            for k in range(1, 3):
                for f in range(4):
                    ins = STT(out=y[:, f, :], in0=conv_in[:, f, k:k + SEQ], scalar=taps[:, 4 * k + f:4 * k + f + 1],
                              in1=y[:, f, :], op0=ALU.mult, op1=ALU.add)
                step(ins)
            for f in range(4):
                b = V[2 + f % 2]
                dve.wait_ge(b.full, b.reads + 1)
                TT(y[:, f, :], y[:, f, :], b.t[:, 0:SEQ], ALU.mult).then_inc(b.free, b.read())

        def linear_attention():
            by_parity = scoreT.rearrange("p t (f m) n -> p m t f n", m=2)
            for m in range(2):
                b = V[m]
                dve.wait_ge(b.full, b.reads + 1)
                TT(by_parity[:, m], b.t[:, :].rearrange("p (t f n) -> p t f n", t=2, f=2),
                   C("chunk_causal").unsqueeze(1).unsqueeze(1).to_broadcast([P, 2, 2, P]), ALU.mult).then_inc(b.free, b.read())
            for w in mark["gv"]:
                dve.wait_ge(*w)
            dve.wait_ge(rope_table.sem, 1)
            n = 0
            for tile in range(2):
                if tile:
                    for w in mark["v_chunk", tile - 1]:
                        dve.wait_ge(*w)
                for c in range(P // GLA_CHUNK):
                    TS(v_chunk[:, c, :], gv[:, tile, :], C("of_chunk")[:, c:c + 1], None, ALU.mult)\
                        .then_inc(v_chunk_done.sem, v_chunk_done.up())
                for half in range(2):
                    for f in range(2):
                        b = V[f]
                        dve.wait_ge(b.full, b.reads + 1)
                        for c in range(4):
                            n = tile * 8 + half * 4 + c
                            u = b.t[:, c * P:(c + 1) * P]
                            if n == 0:
                                ins = nc.vector.tensor_copy(state[f][:, n, :], u)
                            else:
                                ins = STT(out=state[f][:, n, :], in0=state[f][:, n - 1, :], scalar=decay[:, f, n:n + 1],
                                          in1=u, op0=ALU.mult, op1=ALU.add)
                            if c < 3:
                                step(ins)
                        ins.then_inc(b.free, b.read())
                        dve.wait_ge(b.free, b.reads)

        def rope2():
            for x, src in (("q", dqT), ("k", dkT)):
                for i in range(3):
                    for w in mark["d_in", x, i]:
                        dve.wait_ge(*w)
                    for j in range(2):
                        b = V[j]
                        v = src[:, 4 * i + 2 * j:4 * i + 2 * j + 2, :]
                        t2 = tmp[:, :].rearrange("p (f n) -> p f n", f=2)
                        wide = [P, 2, SEQ]
                        dve.wait_ge(b.full, b.reads + 1)
                        TT(t2, b.t[:, :].rearrange("p (f n) -> p f n", f=2), sin2.unsqueeze(1).to_broadcast(wide), ALU.mult)\
                            .then_inc(b.free, b.read())
                        step(TT(v, v, cos2.unsqueeze(1).to_broadcast(wide), ALU.mult))
                        dve.wait_ge(b.free, b.reads)
                        TT(v, v, t2, ALU.add).then_inc(d_rope_done.sem, d_rope_done.up())
                        dve.wait_ge(d_rope_done.sem, d_rope_done.n)

        def linear_attention_out():
            for m in range(2):
                b = V[2 + m]
                o, o_sq = [v.rearrange("p (f m) n -> p m f n", m=2)[:, m] for v in (o2T, o2sq)]
                dve.wait_ge(b.full, b.reads + 1)
                nc.vector.tensor_copy(o, b.t[:, :].rearrange("p (f n) -> p f n", f=2)).then_inc(b.free, b.read())
                dve.wait_ge(b.free, b.reads)
                ins = TT(o_sq, o, o, ALU.mult)
            ins.then_inc(o2sq_done.sem, o2sq_done.up())
            b = V[0]
            dve.wait_ge(b.full, b.reads + 1)
            TS(o2r, b.t[:, 0:2 * GLA_HEADS], 1.0 / P, EPS, ALU.mult, ALU.add).then_inc(b.free, b.read())
            dve.wait_ge(b.free, b.reads)
            power(TS(o2r, o2r, 0.0, None, ALU.add))
            for half in range(2):
                b = V[half]
                o = o2T[:, 2 * half:2 * half + 2, :].rearrange("p h n -> p (h n)")
                dve.wait_ge(b.full, b.reads + 1)
                STT(out=o, in0=o, scalar=col("gla_norm_g"), in1=b.t[:, :], op0=ALU.mult, op1=ALU.mult)\
                    .then_inc(b.free, b.read())
                dve.wait_ge(b.free, b.reads)
            TT(ys2T[:, 0], o2T, g2T, ALU.mult).then_inc(y_gla_done.sem, y_gla_done.up())
            dve.wait_ge(y_gla_done.sem, 1)

        def dilated():
            items = [(tile, hd) for tile in range(2) for hd in range(4)]
            scale = P ** -0.5

            def scored(i):
                tile, hd = items[i]
                n = (tile + 1) * P
                per = min(3, 512 // n)
                for g in range(0, 3, per):
                    m = min(per, 3 - g)
                    b = V[2 * (i % 2) + g // per]
                    dve.wait_ge(b.full, b.reads + 1)
                    STT(out=d_sc[:, i % 2, g * n:(g + m) * n].rearrange("p (g n) -> p g n", g=m),
                        in0=b.t[:, 0:m * n].rearrange("p (g n) -> p g n", g=m), scalar=scale,
                        in1=dil_mask[:, g:g + m, tile, 0:n], op0=ALU.mult, op1=ALU.add).then_inc(b.free, b.read())
                    dve.wait_ge(b.free, b.reads)
                nc.vector.tensor_reduce(d_max[:, i % 2:i % 2 + 1], d_sc[:, i % 2, 0:3 * n], X, ALU.max, negate=True)\
                    .then_inc(d_max_done.sem, d_max_done.up())

            def normed(i):
                n = 3 * (items[i][0] + 1) * P
                inv = d_inv[:, i % 2:i % 2 + 1]
                dve.wait_ge(d_exp_done.sem, i + 1)
                step(nc.vector.reciprocal(inv, d_sum[:, i % 2:i % 2 + 1]))
                TS(d_p[:, i % 2, 0:n], d_p[:, i % 2, 0:n], inv, None, ALU.mult).then_inc(d_p_done.sem, d_p_done.up())

            scored(0)
            for i in range(len(items)):
                if i + 1 < len(items):
                    scored(i + 1)
                normed(i)

        def add_normed(parts, gain):
            for b, tile, half in parts:
                dve.wait_ge(b.full, b.reads + 1)
                nc.vector.tensor_copy(y2[:, tile, half * 512:(half + 1) * 512], b.t[:, :]).then_inc(b.free, b.read())
            root_mean()
            for tile in range(2):
                step(STT(out=y2[:, tile, :], in0=y2[:, tile, :], scalar=rstd[:, tile:tile + 1], in1=gain,
                         op0=ALU.mult, op1=ALU.mult))
                TT(h[:, tile, :], h[:, tile, :], y2[:, tile, :], ALU.add).then_inc(x_done.sem, x_done.up())
                dve.wait_ge(x_done.sem, x_done.n)

        def feed_forward():
            taps = col("ff_conv_w")
            step(nc.vector.memset(gate_in[:, :, 0:2], 0.0))
            turns = Turns((V[0], "reads", 1), (V[1], "reads", 1), (dve_step, "n", 4),
                          (conv_done, "n", 2))
            with dve.Fori(0, UP_CHUNKS) as i:
                turns.turn(i)
                for f in range(2):
                    def tap(k):
                        return taps[:, bass.ds(k * FF_TILES + 2 * i + f, 1)]

                    y = conved[:, f, :]
                    dve.wait_ge(A[f].free, mark["up"][f] + i + 1)
                    step(TS(y, gate_in[:, f, 0:SEQ], tap(0), None, ALU.mult))
                    step(STT(out=y, in0=gate_in[:, f, 1:SEQ + 1], scalar=tap(1), in1=y, op0=ALU.mult, op1=ALU.add))
                    STT(out=y, in0=gate_in[:, f, 2:SEQ + 2], scalar=tap(2), in1=y, op0=ALU.mult, op1=ALU.add)\
                        .then_inc(conv_done.sem, conv_done.up())
                for f in range(2):
                    b = V[f]
                    dve.wait_ge(b.full, b.reads + 1)
                    dve.wait_ge(gelu_done.sem, 2 * i + f + 1)
                    dst = hidden[:, bass.ds(2 * i + f, 1), :].rearrange("p k n -> p (k n)")
                    TT(dst, conved[:, f, :], b.t[:, 0:SEQ], ALU.mult).then_inc(b.free, b.read())
                    dve.wait_ge(b.free, b.reads)
            turns.done(UP_CHUNKS)

        zero_conditions()
        dve.wait_ge(first_loaded, 32)
        dve.wait_ge(setup, 16 * SETUP)
        setup_scalars()
        for l in range(DEPTH):
            modulation(l)
            norm_columns(l)
            projections(l)
            differential(l)
            neighbourhood(l)
            merge(l)
            mix_out(l)
            second_norm(l)
            route(l)
            experts(l)
            combine(l)
        final_norm()
        rows_norm()
        rope_tables()
        forget_gates()
        short_conv()
        linear_attention()
        rope2()
        linear_attention_out()
        dilated()
        merge(DEPTH)
        dve.wait_ge(block2_in[2], 32)
        add_normed([(V[2], 0, 0), (V[3], 1, 0), (V[2], 0, 1), (V[3], 1, 1)], mix_g)
        rows_norm()
        feed_forward()
        add_normed([(V[2 * tile + half], tile, half) for tile in range(2) for half in range(2)], ffn_g)

    @block.gpsimd
    def _(pool):
        def power(out_, in_):
            pool.wait_ge(pow_in.sem, pow_out.n + 1)
            nc.gpsimd.tensor_tensor(out_, in_, C("minus_half")[:, 0:in_.shape[1]], ALU.pow)\
                .then_inc(pow_out.sem, pow_out.up())

        def bias_row(l):
            pool.dma_start(bias_rows, t["b_ada"][l].rearrange("(j n) -> j n", n=COLS)).then_inc(bias_in, 16)

        def rows(l):
            if l >= 1:
                pool.wait_ge(h_done.sem, h_end(l - 1))
            pool.dma_start(sgw[:, :, :], t["sg_w"][l]).then_inc(rows_in[l], 16)
            pool.dma_start(ln_rows[:, 0, :], t["sg_ln_g"][l:l + 1, :].to_broadcast([P, 512])).then_inc(rows_in[l], 16)
            pool.dma_start(ln_rows[:, 1, :], t["sg_ln_b"][l:l + 1, :].to_broadcast([P, 512])).then_inc(rows_in[l], 16)

        def second_modulation(l):
            pool.wait_ge(*mark["attended", l])
            pool.wait_ge(modrow_stored, 32 * (l + 1))
            for dst, kind in ((gt1b, 0), (sh2b, 1), (a2b, 2), (gt2b, 3)):
                src = mod_rows[l][:, kind, :].unsqueeze(0).to_broadcast([P, 2, D])
                pool.dma_start(dst, src).then_inc(mods_in[l], 16)

        def dispatch(l):
            pool.wait_ge(token_done.sem, l + 1)
            pool.wait_ge(x_stored[l], 16 * tiles(l))

        def half_rows(rows):
            return rows.rearrange("t (h n) -> (t h) n", h=2)

        def gather(l, e):
            b = e % 2
            if e >= 2:
                pool.wait_ge(A[1].full, mark["moe", l]["A"][1] + e - 2)
            pool.indirect_dma_start(
                out=xg[:, b, :], out_offset=None, in_=half_rows(x_rows[l][0:tiles(l) * P, :]),
                in_offset=bass.IndirectOffsetOnAxis(ap=token_of[:, e:e + 1], axis=0)).then_inc(gathered[b], 16)

        def scatter(l, e):
            b = e % 2
            base = mark["moe", l]
            pool.wait_ge(V[2 + b].free, base["V"][2 + b] + e // 2 + 1)
            pool.indirect_dma_start(
                out=half_rows(y_rows[l][0:tiles(l) * 2 * P, :]), out_offset=bass.IndirectOffsetOnAxis(ap=table[:, e:e + 1], axis=0),
                in_=y_sb[:, b, :], in_offset=None, bounds_check=tiles(l) * 4 * P - 1, oob_is_err=False)\
                .then_inc(scattered[b], 16)

        def experts(l):
            gather(l, 0)
            gather(l, 1)
            if l < DEPTH - 1:
                pool.wait_ge(xb[l]["list"], 1)
                bias_row(l + 1)
            for e in range(N_EXP):
                if e + 2 < N_EXP:
                    gather(l, e + 2)
                scatter(l, e)
            with further_blocks(pool, l) as j:
                s, r = xb[l], r_area[l]
                pool.wait_ge(s["index"], j + 1)
                pool.sem_inc(s["passed"], 1)
                pool.wait_ge(*mark["moe_end", l])
                pool.indirect_dma_start(
                    out=xg[:, 0, :], out_offset=None, in_=half_rows(x_rows[l][0:tiles(l) * P, :]),
                    in_offset=bass.IndirectOffsetOnAxis(ap=r["x_ids"][:, 0:1], axis=0)).then_inc(s["rows"], 16)
                pool.wait_ge(s["dve"], 2 * j + 2)
                pool.sem_inc(s["passed"], 1)
                pool.indirect_dma_start(
                    out=half_rows(y_rows[l][0:tiles(l) * 2 * P, :]), out_offset=bass.IndirectOffsetOnAxis(ap=r["x_ids"][:, 1:2], axis=0),
                    in_=y_sb[:, 0, :], in_offset=None, bounds_check=tiles(l) * 4 * P - 1, oob_is_err=False)\
                    .then_inc(s["sent"], 16)
                pool.wait_ge(s["sent"], 16 * j + 16)
                pool.sem_inc(s["passed"], 1)

        def results(l):
            for b in range(2):
                pool.wait_ge(scattered[b], 16 * (N_EXP // 2) * (l + 1))
            y2 = y_rows[l].rearrange("(t k) n -> t (k n)", k=2)
            before = h_done_mix(l)
            for tile in range(tiles(l)):
                if tile >= 2:
                    pool.wait_ge(h_done.sem, before + tile - 1)
                pool.dma_start(ybuf[:, tile % 2, :], y2[tile * P:(tile + 1) * P, :]).then_inc(y_in[tile % 2], 16)

        def second_block_early():
            pool.dma_start(const[:, KEPT:KEPT + CONST2.shape[1]], t["const2"]).then_inc(block2_in[0], 16)
            pool.dma_start(w_alow, t["w_alow"]).then_inc(block2_in[0], 16)
            pool.dma_start(w_alpha, t["w_alpha"]).then_inc(block2_in[0], 16)
            pool.wait_ge(h_done.sem, h_done_mix(DEPTH - 1))
            pool.dma_start(final_g, t["g_final"].to_broadcast([P, D])).then_inc(block2_in[1], 16)

        bias_row(0)
        pool.wait_ge(first_loaded, 32)
        pool.wait_ge(setup, 16 * SETUP)
        for l in range(DEPTH):
            rows(l)
            power(rstd[:, :], rstd[:, :])
            pool.wait_ge(*mark["normed", l])
            pool.dma_start(g2row, t["g_norm_ffn"][l:l + 1, :].to_broadcast([2, D])).then_inc(rows_in[l], 16)
            for tile in range(tiles(l)):
                power(ln_r, ln_var)
            pool.wait_ge(modrow_done.sem, l + 1)
            pool.wait_ge(*mark["ada", l])
            for i in range(2):
                pool.dma_start(mod_rows[l][:, 2 * i:2 * i + 2, :].rearrange("s k n -> s (k n)"),
                               branches[0:2, 4096 * i:4096 * i + 2 * D]).then_inc(modrow_stored, 16)
            for tile in range(tiles(l)):
                power(head_r, head_sq)
            second_modulation(l)
            power(rstd[:, 0:tiles(l)], rstd[:, 0:tiles(l)])
            dispatch(l)
            if l == DEPTH - 1:
                second_block_early()
            experts(l)
            results(l)
        pool.wait_ge(*mark["moe_end", DEPTH - 1])
        pool.dma_start(dil_mask.rearrange("p d t n -> p (d t n)"), t["dil_masks"]).then_inc(block2_in[0], 16)
        pool.dma_start(pos_i, t["positions"].to_broadcast([P, SEQ])).then_inc(block2_in[1], 16)
        power(rstd[:, 0:2], rstd[:, 0:2])
        power(rstd[:, 0:2], rstd[:, 0:2])
        power(o2r, o2r)
        pool.wait_ge(*mark["attended", 2])
        for dst, name in ((mix_g, "post_mix_g"), (ffn_g, "post_ffn_g")):
            pool.dma_start(dst, t[name].to_broadcast([P, D])).then_inc(block2_in[2], 16)
        power(rstd[:, 0:2], rstd[:, 0:2])
        power(rstd[:, 0:2], rstd[:, 0:2])
        power(rstd[:, 0:2], rstd[:, 0:2])

    @block.sync
    def _(sp):
        def source(c):
            kind, l, j = c
            if kind == "ada":
                return t["w_ada"][l, j]
            if kind == "in":
                return t["w_in"][l, W_IN_BLOCKS.index(j)]
            if kind == "in2":
                return t["w_in2"][IN2_ORDER.index(j)]
            if kind == "up":
                return t["w_up"][j]
            if kind == "down":
                return t["w_down"][j, :, 0:min(DOWN_K, FF_TILES - j * DOWN_K) * D]
            return t[{"bias": "na_bias", "merge": "w_merge", "out": "w_out"}[kind]][l, j]

        def last_read(c):
            kind, l, j = c
            if kind == "merge":
                n = N_BR * j + 2
                return V[n % 2].full, mark["merge", l][2 + n % 2] + n // 2 + 1
            if kind == "up":
                return V[1].full, mark["up"][3] + j + 1
            if kind == "expert":
                return expert_read(l, j // 3, (j // 3) % 2, j // 3 // 2, j % 3)
            return mark[("used",) + c]

        def expert_read(l, e, parity, e_half, r):
            base = mark["moe", l]
            if r == 0:
                return S[parity].full, base["S"][parity] + e_half + 1
            if r == 1:
                return V[parity].full, base["V"][parity] + e_half + 1
            return V[2 + parity].full, base["V"][2 + parity] + e_half + 1

        def load(c):
            n = PLACE[c]
            if n >= NSLOT:
                sp.wait_ge(*last_read(ORDER[n - NSLOT]))
            src = source(c)
            sp.dma_start(ring[n % NSLOT][:, 0:src.shape[1]], src).then_inc(ring_loaded[n % NSLOT], 16)

        def load_more(c):
            _, l, d = c
            first = PLACE["merge", l, 0]
            if d < NSLOT - 1:
                return
            for dd in range(NSLOT) if d == NSLOT - 1 else [d]:
                s = (first + dd) % NSLOT
                if dd == 0:
                    sp.wait_ge(*mark["attended", l])
                if dd >= NSLOT:
                    sp.wait_ge(*last_read(("merge", l, dd - NSLOT)))
                sp.dma_start(more[:, s, :], t["w_more"][l, dd]).then_inc(more_loaded[s], 16)

        def load_setup():
            sp.dma_start(h[:, 0:2, :], t["x"][0].rearrange("(t p) n -> p t n", p=P)).then_inc(setup, 16)
            sp.dma_start(h[:, 2:4, :], t["ctx"][0].rearrange("(t p) n -> p t n", p=P)).then_inc(setup, 16)
            sp.dma_start(wr[:, :, :, :], t["w_route"]).then_inc(setup, 16)
            sp.dma_start(rb[:, :, :], t["b_route"]).then_inc(setup, 16)
            sp.dma_start(lam_in[:, :, :, :], t["da_lambda"].unsqueeze(0).to_broadcast([P, DEPTH, 4, 64])).then_inc(setup, 16)

        sp.dma_start(cols[:, :], t["cols"]).then_inc(first_loaded, 16)
        load(ORDER[0])
        sp.dma_start(const[:, :], t["const"]).then_inc(first_loaded, 16)
        for c in ORDER[1:NSLOT]:
            load(c)
        load_setup()

        def experts(l):
            for e in range(MOE_AHEAD):
                for r in range(3):
                    n = PLACE["expert", l, 3 * e + r]
                    sp.wait_ge(*last_read(ORDER[n - NSLOT]))
                    sp.dma_start(ring[n % NSLOT][:, 0:4096], t["w_moe"][l, e, r]).then_inc(ring_loaded[n % NSLOT], 16)
            with sp.Fori(1, N_EXP // MOE_AHEAD) as i:
                for q in range(MOE_AHEAD):
                    for r in range(3):
                        n = PLACE["expert", l, 3 * q + r]
                        back = 1 if r >= 1 else 2
                        sp.wait_ge(*expert_read(l, MOE_AHEAD * i + (q - back), (q - back) % 2,
                                                2 * i + (q - back) // 2, (r + 2) % 3))
                        src = t["w_moe"][l, bass.ds(MOE_AHEAD * i + q, 1), r].rearrange("e p n -> (e p) n")
                        sp.dma_start(ring[n % NSLOT][:, 0:4096], src).then_inc(ring_loaded[n % NSLOT], 16)
            with further_blocks(sp, l) as j:
                s = xb[l]
                e = sp.value_load(r_area[l]["x_list"][:, bass.ds(2 * j + 1, 1)], min_val=0, max_val=N_EXP - 1)
                sp.wait_ge(*mark["moe_end", l])
                for r in range(3):
                    src = t["w_moe"][l, bass.ds(e, 1), r].rearrange("e p n -> (e p) n")
                    sp.dma_start(ring[r][:, 0:4096], src).then_inc(s["weights"], 16)
                sp.wait_ge(s["pe"], 4 * j + 4)
                sp.sem_inc(s["passed"], 1)

        for l in range(DEPTH):
            stages = (("ada", "in"), ("bias",), ("merge", "out"))
            for i, kinds in enumerate(stages):
                for c in ORDER:
                    if c[1] == l and c[0] in kinds and PLACE[c] >= NSLOT:
                        load(c)
                        if c[0] == "merge":
                            load_more(c)
            experts(l)

        for i, kinds in enumerate((("in2",), ("merge", "out"), ("up", "down"))):
            for c in ORDER:
                if c[1] == 2 and c[0] in kinds:
                    load(c)
                    if c[0] == "merge":
                        load_more(c)
        sp.wait_ge(x_done.sem, 4)
        sp.dma_start(out[0].rearrange("(t p) n -> p t n", p=P), h[:, 0:2, :]).then_inc(out_stored, 16)
        sp.wait_ge(out_stored, 16)


def columns(v):
    return np.ascontiguousarray(np.asarray(v).reshape(-1, P).T)


def column_table(a):
    at, parts = {}, []

    def put(name, v):
        at[name] = (sum(p.shape[1] for p in parts), v.shape[1])
        parts.append(v)

    c, cc = columns(a["c"][0]), columns(a["c_ctx"])
    put("cond", np.stack([c, cc], axis=2).reshape(P, 2 * KD))
    for l in range(DEPTH):
        put(f"g1{l}", columns(a["g_norm_mix"][l]))
        put(f"sub_g{l}", columns(a["da_subln_g"][l]))
        put(f"sg_b{l}", np.ascontiguousarray(a["sg_b"][l].T))
    put("b_alpha", columns(a["b_alpha_2"][0]))
    put("gla_norm_g", columns(a["gla_norm_g_2"][0]))
    put("sc_conv_w", columns(a["sc_conv_w_2"][0]))
    put("b_gate", columns(a["b_gate_2"][0]))
    put("ff_conv_w", columns(a["ff_conv_w_2"][0]))
    put("ff_conv_b", columns(a["ff_conv_b_2"][0]))
    put("pre_mix_g", columns(a["pre_mix_g_2"][0]))
    put("pre_ffn_g", columns(a["pre_ffn_g_2"][0]))
    return np.ascontiguousarray(np.concatenate(parts, axis=1)), at


SECOND_COLUMNS = {"b_alpha": 2 * P, "gla_norm_g": P, "sc_conv_w": 3 * 4 * P, "b_gate": N_BR * D, "ff_conv_w": 3 * D_FF,
                  "ff_conv_b": D_FF, "pre_mix_g": D, "pre_ffn_g": D}
COLS_AT = column_table({
    **{f"{n}_2": np.zeros((1, size), np.float32) for n, size in SECOND_COLUMNS.items()},
    "c": np.zeros((1, D), np.float32), "c_ctx": np.zeros(D, np.float32), "g_norm_mix": np.zeros((DEPTH, D), np.float32),
    "da_subln_g": np.zeros((DEPTH, P), np.float32), "sg_b": np.zeros((DEPTH, 4, P), np.float32)})[1]


def chunks(w):
    k, n = w.shape[0] // P, w.shape[1] // COLS
    return np.ascontiguousarray(w.reshape(k, P, n, COLS).transpose(2, 1, 0, 3).reshape(n, P, k * COLS))


def by_partition(w):
    k = w.shape[-2] // P
    v = w.reshape(w.shape[:-2] + (k, P, w.shape[-1]))
    v = np.moveaxis(v, -3, -2)
    return v.reshape(w.shape[:-2] + (P, k * w.shape[-1]))


def neighbourhood_bias(rpb):
    col = np.arange(GRID_W)
    start = np.clip(col - NA_COLS // 2, 0, GRID_W - NA_COLS)
    inside = (col[None, :] >= start[:, None]) & (col[None, :] < start[:, None] + NA_COLS)
    dc = np.where(inside, col[None, :] - col[:, None] + NA_COLS - 1, 2 * NA_COLS - 1)
    dr = np.arange(ROWS)[None, :] - np.arange(ROWS)[:, None] + NA_ROWS - 1
    padded = np.pad(rpb, ((0, 0), (0, 0), (0, 1)), constant_values=NEG)
    full = padded[:, dr[:, None, :, None], dc[None, :, None, :]].reshape(rpb.shape[0], SEQ, SEQ)
    return full.reshape(rpb.shape[0], 2, P, SEQ).transpose(2, 0, 1, 3).reshape(P, -1)


def merge_chunks(w_gate, w_branch):
    n = w_gate.shape[0]
    gates = w_gate.reshape(n, KD, P, N_BR, MERGE_CHUNKS, P).transpose(0, 4, 2, 3, 1, 5)
    br = w_branch.reshape(n, N_BR, 4, P, MERGE_CHUNKS, P).transpose(0, 4, 3, 1, 2, 5)
    return np.concatenate([gates.reshape(n, MERGE_CHUNKS, P, -1), br.reshape(n, MERGE_CHUNKS, P, -1)], axis=3)


def second_layouts(a):
    m = {"const2": CONST2, "dil_masks": DIL_MASKS.reshape(P, -1), "positions": a["positions_2"], "g_final": a["g_final"][None]}
    m["post_mix_g"], m["post_ffn_g"] = a["post_mix_g_2"], a["post_ffn_g_2"]
    w = a["w_in_2"][0]
    m["w_in2"] = np.stack([by_partition(w[:, IN2_AT[n]:IN2_AT[n] + COLS]) for n in IN2_ORDER])
    m["w_alow"] = by_partition(w[:, ALOW_AT:ALOW_AT + GLA_RANK]).reshape(P, KD, GLA_RANK)
    m["w_alpha"] = a["w_alpha_up_2"][0]
    up = np.stack([a["w_ff_gate_2"][0], a["w_ff_up_2"][0]])
    m["w_up"] = up.reshape(2, KD, P, UP_CHUNKS, 2 * P).transpose(3, 2, 1, 0, 4).reshape(UP_CHUNKS, P, SLOT)
    down = by_partition(np.pad(a["w_ff_down_2"][0], ((0, DOWN_CHUNKS * DOWN_K * P - D_FF), (0, 0))))
    m["w_down"] = down.reshape(P, DOWN_CHUNKS, DOWN_K * D).transpose(1, 0, 2)
    return m


def layouts(a):
    m = second_layouts(a)
    m["x"], m["ctx"] = a["x"], a["ctx"]
    m["const"] = CONST
    m["cols"] = column_table(a)[0]
    for n in ("b_ada", "g_norm_ffn", "sg_ln_g", "sg_ln_b", "da_lambda"):
        m[n] = a[n]
    m["w_ada"] = np.stack([chunks(w) for w in a["w_ada"]])
    m["w_in"] = np.stack([chunks(w[:, :8 * COLS]) for w in a["w_in"]])
    m["na_bias"] = np.stack([neighbourhood_bias(r) for r in a["na_rpb"]])[:, None]
    w_merge = merge_chunks(a["w_in"][:, :, 8 * COLS:], a["w_branch"])
    w_merge = np.concatenate([w_merge, merge_chunks(a["w_gate_2"], a["w_branch_2"])])
    m["w_merge"], m["w_more"] = w_merge[..., :SLOT], w_merge[..., SLOT:]
    m["w_out"] = np.stack([chunks(w) for w in (*a["w_out"], a["w_mix_out_2"][0])])
    m["sg_w"] = a["sg_w"].transpose(0, 3, 1, 2)
    m["w_route"] = by_partition(np.concatenate([a["moe_w_group"], a["moe_w_router"]], axis=2))\
        .transpose(1, 0, 2).reshape(P, DEPTH, KD, 36)
    m["b_route"] = np.concatenate([a["moe_b_group"], a["moe_b_router"]], axis=1)[None]
    m["w_moe"] = np.stack([by_partition(a["moe_w_gate"]), by_partition(a["moe_w_up"]), by_partition(a["moe_w_down"])], axis=2)
    return {k: np.ascontiguousarray(v) for k, v in m.items()}


def kernel(**inputs):
    import concourse.bacc as bacc
    from concourse.bass_utils import run_bass_kernel_spmd

    m = layouts({k: np.asarray(v) for k, v in inputs.items()})
    nc = bacc.Bacc("TRN2", target_bir_lowering=False, num_devices=1)
    t = {k: nc.dram_tensor(f"in_{k}", v.shape, mybir.dt.from_np(v.dtype), kind="ExternalInput").ap() for k, v in m.items()}
    out = nc.dram_tensor("out", (1, SEQ, D), F32, kind="ExternalOutput").ap()
    program(nc, t, out)
    r = run_bass_kernel_spmd(nc, [{f"in_{k}": v for k, v in m.items()}], core_ids=[0])
    return r.results[0]["out"]
```
